# Optimizing a Trainium2 kernel written in Bass

```python
import math
import jax, jax.numpy as jnp
from jax import lax
import numpy as np

D_MODEL = 1024
BATCH = 1
SEQ = 512
DEPTH = 2
DEC_BATCH = 1
DEC_SEQ = 1024
PAST_LEN = 128

EPS = 1e-6
N_EVEN = (DEPTH + 1) // 2
N_ODD = DEPTH // 2
W_A = D_MODEL
S5_GROUP = 16
S5_GROUPS = W_A // S5_GROUP
S5_STATE = 64
MLA_HEADS = D_MODEL // 128
MLA_NOPE = 128
MLA_ROPE = 64
MLA_V = 128
W_B = MLA_HEADS * MLA_V
Q_LORA = (3 * D_MODEL) // 8
KV_LORA = D_MODEL // 4
ROPE_THETA = 10000.0
Q_BLOCK = 128
MLA_SCALE = (MLA_NOPE + MLA_ROPE) ** -0.5
W_C = D_MODEL
MLSTM_HEADS = 4
MLSTM_DH = W_C // MLSTM_HEADS
CONV_WIDTH = 3
CONV_PAD = CONV_WIDTH // 2
W_D = D_MODEL
GLA_HEADS = 4
GLA_DK_TOTAL = W_D // 2
GLA_DK = GLA_DK_TOTAL // GLA_HEADS
GLA_DV = W_D // GLA_HEADS
GATE_RANK = 16
GATE_TAU = 16.0
CHUNK = 64

EVEN_SPLITS = (W_A, W_A, Q_LORA, KV_LORA, MLA_ROPE, W_B)
IN_EVEN = sum(EVEN_SPLITS)
ODD_SPLITS = (W_C, W_C, W_C, W_C, 4 * MLSTM_HEADS, GLA_DK_TOTAL, GLA_DK_TOTAL, W_D, W_D, 2 * GATE_RANK)
IN_ODD = sum(ODD_SPLITS)

kernel_name = "hybrid_bidir_s5_mla_mlstm_gla_encoder"

F32 = jnp.float32

def _rms(x, g):
    xf = x.astype(F32)
    y = xf * lax.rsqrt(jnp.mean(xf * xf, axis=-1, keepdims=True) + EPS)
    return (y * g.astype(F32)).astype(x.dtype)

def _head_rms(x, g, dtype):
    xf = x.astype(F32)
    y = xf * lax.rsqrt(jnp.mean(xf * xf, axis=-1, keepdims=True) + EPS)
    y = y * g.astype(F32).reshape(x.shape[-2], x.shape[-1])
    return y.reshape(x.shape[0], x.shape[1], -1).astype(dtype)

def _split(x, sizes):
    idx = [int(i) for i in np.cumsum(sizes)[:-1]]
    return jnp.split(x, idx, axis=-1)

def _flip(t):
    return jnp.flip(t, axis=2)

def _diag_scan(lam_bar, bu, reverse):
    L = bu.shape[1]
    a = jnp.broadcast_to(lam_bar, (L,) + lam_bar.shape)

    def binop(e1, e2):
        a1, b1 = e1
        a2, b2 = e2
        return a2 * a1, a2 * b1 + b2

    def one(bseq):
        return lax.associative_scan(binop, (a, bseq), reverse=reverse)[1]

    return jax.vmap(one)(bu)

def _s5(u, lam_re, lam_im, log_dt, b_re, b_im, c_re, c_im, d_skip):
    bsz, L, W = u.shape
    uf = u.astype(F32)
    ug = uf.reshape(bsz, L, S5_GROUPS, S5_GROUP)
    y = uf * d_skip.astype(F32)
    for d in range(2):
        lam = lax.complex(jnp.minimum(lam_re[d].astype(F32), -1e-4), lam_im[d].astype(F32))
        dt = jnp.exp(log_dt[d].astype(F32))[:, None]
        lam_bar = jnp.exp(lam * dt)
        b = lax.complex(b_re[d].astype(F32), b_im[d].astype(F32))
        b_bar = ((lam_bar - 1.0) / lam)[..., None] * b
        bu = jnp.einsum('blgc,gpc->blgp', ug, b_bar)
        xs = _diag_scan(lam_bar, bu, reverse=(d == 1))
        c = lax.complex(c_re[d].astype(F32), c_im[d].astype(F32))
        y = y + jnp.real(jnp.einsum('blgp,gcp->blgc', xs, c)).reshape(bsz, L, W)
    return y.astype(u.dtype)

def _rope_tables(L):
    inv = ROPE_THETA ** (-jnp.arange(0, MLA_ROPE, 2, dtype=F32) / MLA_ROPE)
    ang = jnp.arange(L, dtype=F32)[:, None] * inv[None, :]
    return jnp.cos(ang), jnp.sin(ang)

def _rope(x, cos, sin):
    half = x.shape[-1] // 2
    x1, x2 = x[..., :half], x[..., half:]
    cos = cos.astype(x.dtype)
    sin = sin.astype(x.dtype)
    return jnp.concatenate([x1 * cos - x2 * sin, x1 * sin + x2 * cos], axis=-1)

def _mla(c_q, c_kv, k_rope, q_norm, w_uq, kv_norm, w_ukv):
    bsz, L, _ = c_q.shape
    q = (_rms(c_q, q_norm) @ w_uq).reshape(bsz, L, MLA_HEADS, MLA_NOPE + MLA_ROPE)
    q_nope, q_rope = q[..., :MLA_NOPE], q[..., MLA_NOPE:]
    kv = (_rms(c_kv, kv_norm) @ w_ukv).reshape(bsz, L, MLA_HEADS, MLA_NOPE + MLA_V)
    k_nope, v = kv[..., :MLA_NOPE], kv[..., MLA_NOPE:]
    cos, sin = _rope_tables(L)
    q_rope = _rope(q_rope, cos[:, None, :], sin[:, None, :])
    k_rope = _rope(k_rope, cos, sin)
    nb = L // Q_BLOCK
    qn_b = q_nope.reshape(bsz, nb, Q_BLOCK, MLA_HEADS, MLA_NOPE).swapaxes(0, 1)
    qr_b = q_rope.reshape(bsz, nb, Q_BLOCK, MLA_HEADS, MLA_ROPE).swapaxes(0, 1)

    def block(args):
        qn, qr = args
        s = (jnp.einsum('bqhd,bkhd->bhqk', qn, k_nope) + jnp.einsum('bqhd,bkd->bhqk', qr, k_rope)).astype(F32) * MLA_SCALE
        p = jax.nn.softmax(s, axis=-1).astype(v.dtype)
        return jnp.einsum('bhqk,bkhd->bqhd', p, v)

    o = lax.map(block, (qn_b, qr_b))
    return o.swapaxes(0, 1).reshape(bsz, L, W_B)

def _mlstm_dir(q, k, v, li, lf):
    q, k, v = q.astype(F32), k.astype(F32), v.astype(F32)
    bsz, H, L, dk = q.shape
    dv = v.shape[-1]
    nc = L // CHUNK

    def rs(t):
        return jnp.moveaxis(t.reshape(bsz, H, nc, CHUNK, *t.shape[3:]), 2, 0)

    causal = jnp.tril(jnp.ones((CHUNK, CHUNK), dtype=bool))

    def step(carry, inp):
        C, n, m = carry
        qb, kb, vb, ib, fb = inp
        b = jnp.cumsum(fb, axis=-1)
        d = jnp.where(causal, b[..., :, None] - b[..., None, :] + ib[..., None, :], -jnp.inf)
        inter = b + m[..., None]
        m_t = jnp.maximum(inter, jnp.max(d, axis=-1))
        s = jnp.einsum('bhtd,bhsd->bhts', qb, kb) * jnp.exp(d - m_t[..., None])
        a = jnp.exp(inter - m_t)
        num = jnp.einsum('bhts,bhsv->bhtv', s, vb) + a[..., None] * jnp.einsum('bhtd,bhdv->bhtv', qb, C)
        den = jnp.sum(s, axis=-1) + a * jnp.einsum('bhtd,bhd->bht', qb, n)
        h = num / jnp.maximum(jnp.abs(den), jnp.exp(-m_t))[..., None]
        bT = b[..., -1]
        g = bT[..., None] - b + ib
        m_new = jnp.maximum(bT + m, jnp.max(g, axis=-1))
        wk = jnp.exp(g - m_new[..., None])
        decay = jnp.exp(bT + m - m_new)
        C = decay[..., None, None] * C + jnp.einsum('bhs,bhsd,bhsv->bhdv', wk, kb, vb)
        n = decay[..., None] * n + jnp.einsum('bhs,bhsd->bhd', wk, kb)
        return (C, n, m_new), h

    init = (jnp.zeros((bsz, H, dk, dv), F32), jnp.zeros((bsz, H, dk), F32), jnp.zeros((bsz, H), F32))
    _, hs = lax.scan(step, init, (rs(q), rs(k), rs(v), rs(li), rs(lf)))
    return jnp.moveaxis(hs, 0, 2).reshape(bsz, H, L, dv)

def _gla_dir(q, k, v, lg):
    q, k, v = q.astype(F32), k.astype(F32), v.astype(F32)
    bsz, H, L, dk = q.shape
    dv = v.shape[-1]
    nc = L // CHUNK

    def rs(t):
        return jnp.moveaxis(t.reshape(bsz, H, nc, CHUNK, *t.shape[3:]), 2, 0)

    mask = jnp.tril(jnp.ones((CHUNK, CHUNK), dtype=bool))[..., None]

    def step(S, inp):
        qb, kb, vb, gb = inp
        cb = jnp.cumsum(gb, axis=-2)
        diff = jnp.where(mask, cb[..., :, None, :] - cb[..., None, :, :], -jnp.inf)
        att = jnp.einsum('bhtd,bhsd,bhtsd->bhts', qb, kb, jnp.exp(diff))
        o = jnp.einsum('bhts,bhsv->bhtv', att, vb) + jnp.einsum('bhtd,bhdv->bhtv', qb * jnp.exp(cb), S)
        cT = cb[..., -1:, :]
        S = jnp.exp(cT[..., 0, :])[..., None] * S + jnp.einsum('bhsd,bhsv->bhdv', kb * jnp.exp(cT - cb), vb)
        return S, o

    _, os_ = lax.scan(step, jnp.zeros((bsz, H, dk, dv), F32), (rs(q), rs(k), rs(v), rs(lg)))
    return jnp.moveaxis(os_, 0, 2).reshape(bsz, H, L, dv)

def _even_mixer(h, w_in, lam_re, lam_im, log_dt, b_re, b_im, c_re, c_im, d_skip, w_glu,
                q_norm, w_uq, kv_norm, w_ukv, w_out):
    u_a, z_a, c_q, c_kv, k_rope, z_b = _split(h @ w_in, EVEN_SPLITS)
    g = jax.nn.gelu(_s5(u_a, lam_re, lam_im, log_dt, b_re, b_im, c_re, c_im, d_skip))
    y_a = g * jax.nn.sigmoid(g @ w_glu) * jax.nn.silu(z_a)
    y_b = _mla(c_q, c_kv, k_rope, q_norm, w_uq, kv_norm, w_ukv) * jax.nn.silu(z_b)
    return jnp.concatenate([y_a, y_b], axis=-1) @ w_out

def _odd_mixer(h, w_in, conv_w, conv_b, w_q, w_k, gate_b, c_norm, w_gate2, gate2_b, d_norm, w_out):
    bsz, L, _ = h.shape
    u_c, v_c, o_c, z_c, g_c, q_d, k_d, v_d, z_d, lr_d = _split(h @ w_in, ODD_SPLITS)
    conv = lax.conv_general_dilated(u_c, conv_w[:, None, :].astype(u_c.dtype), (1,), [(CONV_PAD, CONV_PAD)],
                                    dimension_numbers=('NWC', 'WIO', 'NWC'), feature_group_count=W_C)
    a = jax.nn.silu(conv + conv_b).reshape(bsz, L, MLSTM_HEADS, MLSTM_DH)
    q = jnp.einsum('blhd,hde->bhle', a, w_q)
    k = jnp.einsum('blhd,hde->bhle', a, w_k) * (MLSTM_DH ** -0.5)
    v = v_c.reshape(bsz, L, MLSTM_HEADS, MLSTM_DH).transpose(0, 2, 1, 3)
    gates = (g_c + gate_b).astype(F32).reshape(bsz, L, 4, MLSTM_HEADS).transpose(2, 0, 3, 1)
    i_f, f_f, i_b, f_b = gates[0], gates[1], gates[2], gates[3]
    h_f = _mlstm_dir(q, k, v, i_f, jax.nn.log_sigmoid(f_f))
    h_b = _flip(_mlstm_dir(_flip(q), _flip(k), _flip(v), _flip(i_b), _flip(jax.nn.log_sigmoid(f_b))))
    y_c = jax.nn.sigmoid(o_c) * _head_rms((h_f + h_b).transpose(0, 2, 1, 3), c_norm, h.dtype) * jax.nn.silu(z_c)
    qg = q_d.reshape(bsz, L, GLA_HEADS, GLA_DK).transpose(0, 2, 1, 3) * (GLA_DK ** -0.5)
    kg = k_d.reshape(bsz, L, GLA_HEADS, GLA_DK).transpose(0, 2, 1, 3)
    vg = v_d.reshape(bsz, L, GLA_HEADS, GLA_DV).transpose(0, 2, 1, 3)
    lr = lr_d.reshape(bsz, L, 2, GATE_RANK)
    lgs = []
    for d in range(2):
        pre = (lr[:, :, d] @ w_gate2[d] + gate2_b[d]).astype(F32)
        lgs.append((jax.nn.log_sigmoid(pre) / GATE_TAU).reshape(bsz, L, GLA_HEADS, GLA_DK).transpose(0, 2, 1, 3))
    o_f = _gla_dir(qg, kg, vg, lgs[0])
    o_b = _flip(_gla_dir(_flip(qg), _flip(kg), _flip(vg), _flip(lgs[1])))
    y_d = _head_rms((o_f + o_b).transpose(0, 2, 1, 3), d_norm, h.dtype) * jax.nn.silu(z_d)
    return jnp.concatenate([y_c, y_d], axis=-1) @ w_out

def _trunk(x, pre_norm, post_norm, even_params, odd_params):
    for layer in range(DEPTH):
        h = _rms(x, pre_norm[layer])
        j = layer // 2
        if layer % 2 == 0:
            m = _even_mixer(h, *[p[j] for p in even_params])
        else:
            m = _odd_mixer(h, *[p[j] for p in odd_params])
        x = x + _rms(m, post_norm[layer])
    return x

def setup_inputs(seed: int = 0) -> dict:
    key = jax.random.key(seed)
    keys = iter(jax.random.split(key, 48))

    def nrm(shape, scale):
        return jax.random.normal(next(keys), shape, F32) * scale

    G, P, GC = S5_GROUPS, S5_STATE, S5_GROUP
    lam_im = jnp.broadcast_to(jnp.pi * jnp.arange(P, dtype=F32), (N_EVEN, 2, G, P)) + nrm((N_EVEN, 2, G, P), 0.01)
    log_dt = jax.random.uniform(next(keys), (N_EVEN, 2, G), F32, math.log(1e-3), math.log(1e-1))
    gate_base = jnp.stack([jnp.zeros((MLSTM_HEADS,), F32), jnp.linspace(3.0, 6.0, MLSTM_HEADS, dtype=F32),
                           jnp.zeros((MLSTM_HEADS,), F32), jnp.linspace(3.0, 6.0, MLSTM_HEADS, dtype=F32)])
    return {
        "x_prompt": nrm((BATCH, SEQ, D_MODEL), 1.0),
        "x_sample": nrm((DEC_BATCH, DEC_SEQ, D_MODEL), 1.0),
        "pre_norm": 1.0 + nrm((DEPTH, D_MODEL), 0.05),
        "post_norm": 1.0 + nrm((DEPTH, D_MODEL), 0.05),
        "e_w_in": nrm((N_EVEN, D_MODEL, IN_EVEN), D_MODEL ** -0.5),
        "e_lam_re": -0.5 + nrm((N_EVEN, 2, G, P), 0.01),
        "e_lam_im": lam_im,
        "e_log_dt": log_dt,
        "e_b_re": nrm((N_EVEN, 2, G, P, GC), (2 * GC) ** -0.5),
        "e_b_im": nrm((N_EVEN, 2, G, P, GC), (2 * GC) ** -0.5),
        "e_c_re": nrm((N_EVEN, 2, G, GC, P), P ** -0.5),
        "e_c_im": nrm((N_EVEN, 2, G, GC, P), P ** -0.5),
        "e_d_skip": nrm((N_EVEN, W_A), 1.0),
        "e_w_glu": nrm((N_EVEN, W_A, W_A), W_A ** -0.5),
        "e_q_norm": 1.0 + nrm((N_EVEN, Q_LORA), 0.05),
        "e_w_uq": nrm((N_EVEN, Q_LORA, MLA_HEADS * (MLA_NOPE + MLA_ROPE)), Q_LORA ** -0.5),
        "e_kv_norm": 1.0 + nrm((N_EVEN, KV_LORA), 0.05),
        "e_w_ukv": nrm((N_EVEN, KV_LORA, MLA_HEADS * (MLA_NOPE + MLA_V)), KV_LORA ** -0.5),
        "e_w_out": nrm((N_EVEN, W_A + W_B, D_MODEL), (W_A + W_B) ** -0.5),
        "o_w_in": nrm((N_ODD, D_MODEL, IN_ODD), D_MODEL ** -0.5),
        "o_conv_w": nrm((N_ODD, CONV_WIDTH, W_C), CONV_WIDTH ** -0.5),
        "o_conv_b": nrm((N_ODD, W_C), 0.02),
        "o_w_q": nrm((N_ODD, MLSTM_HEADS, MLSTM_DH, MLSTM_DH), MLSTM_DH ** -0.5),
        "o_w_k": nrm((N_ODD, MLSTM_HEADS, MLSTM_DH, MLSTM_DH), MLSTM_DH ** -0.5),
        "o_gate_b": (gate_base[None] + nrm((N_ODD, 4, MLSTM_HEADS), 0.1)).reshape(N_ODD, 4 * MLSTM_HEADS),
        "o_c_norm": 1.0 + nrm((N_ODD, W_C), 0.05),
        "o_w_gate2": nrm((N_ODD, 2, GATE_RANK, GLA_DK_TOTAL), GATE_RANK ** -0.5),
        "o_gate2_b": nrm((N_ODD, 2, GLA_DK_TOTAL), 0.1),
        "o_d_norm": 1.0 + nrm((N_ODD, W_D), 0.05),
        "o_w_out": nrm((N_ODD, W_C + W_D, D_MODEL), (W_C + W_D) ** -0.5),
    }

def reference(x_prompt, x_sample, pre_norm, post_norm, e_w_in, e_lam_re, e_lam_im, e_log_dt, e_b_re, e_b_im,
              e_c_re, e_c_im, e_d_skip, e_w_glu, e_q_norm, e_w_uq, e_kv_norm, e_w_ukv, e_w_out, o_w_in, o_conv_w,
              o_conv_b, o_w_q, o_w_k, o_gate_b, o_c_norm, o_w_gate2, o_gate2_b, o_d_norm, o_w_out):
    even_params = (e_w_in, e_lam_re, e_lam_im, e_log_dt, e_b_re, e_b_im, e_c_re, e_c_im, e_d_skip, e_w_glu,
                   e_q_norm, e_w_uq, e_kv_norm, e_w_ukv, e_w_out)
    odd_params = (o_w_in, o_conv_w, o_conv_b, o_w_q, o_w_k, o_gate_b, o_c_norm, o_w_gate2, o_gate2_b, o_d_norm, o_w_out)
    y_prompt = _trunk(x_prompt, pre_norm, post_norm, even_params, odd_params)
    y_sample = _trunk(x_sample, pre_norm, post_norm, even_params, odd_params)
    return (y_prompt, y_sample)


_drawn_inputs = setup_inputs


def setup_inputs(seed=0):
    import zlib

    import numpy as np

    out = dict(_drawn_inputs(seed))
    spreads = {}
    factors = {'e_lam_re': 8.0,
     'e_q_norm': 4.081,
     'o_conv_b': 3.277,
     'o_c_norm': 4.019,
     'o_gate2_b': 2.845}
    for name, (base, spread) in spreads.items():
        noise = np.random.default_rng([zlib.crc32(name.encode()), seed]).standard_normal(out[name].shape)
        drawn = base * np.exp(spread * noise) if base else spread * noise
        out[name] = __import__('jax').numpy.asarray(drawn.astype(out[name].dtype))
    for name, factor in factors.items():
        out[name] = (out[name] * factor).astype(out[name].dtype)
    return out
```

```python
from contextlib import ExitStack
import math

import numpy as np
import concourse.bass as bass
from concourse import mybir

F32 = mybir.dt.float32
F32R = mybir.dt.float32r
ALU = mybir.AluOpType
ACT = mybir.ActivationFunctionType
AX_X = mybir.AxisListType.X

P = 128
D = 1024
KT = D // P
LP, LS = 512, 1024
T = LP + LS
NT = T // P
SEQS = ((0, LP), (LP, LS))
EPS = 1e-6
W256 = 256

IN_EVEN = 3776
E_U, E_ZA, E_CQ, E_ZB = 0, 1024, 2048, 2752
QL, KVL, ROPE = 384, 256, 64
CW = QL + KVL + ROPE
HEADS, NOPE, VD = 8, 128, 128
MLA_SCALE = (NOPE + ROPE) ** -0.5
G5, GC, ST = 64, 16, 64
CH = 8
NCS, NCP = LS // CH, LP // CH

IN_ODD = 7216
O_U, O_V, O_O, O_Z, O_G, O_Q, O_K, O_VD, O_ZD, O_LR = 0, 1024, 2048, 3072, 4096, 4112, 4624, 5136, 6160, 7184
MH, MD = 4, 256
GH, GK, GV = 4, 128, 256


def bc(ap, dim, n):
    a = ap.unsqueeze(dim)
    shape = list(a.shape)
    shape[dim] = n
    return a.broadcast_to(shape)


class Stage:

    def __init__(self, nc, tag):
        self.nc, self.tag, self.ctx, self.sems = nc, tag, ExitStack(), []

    def __enter__(self):
        return self

    def __exit__(self, *a):
        for x in self.sems:
            self.nc.sync.sem_clear(x)
        self.ctx.close()

    def sb(self, name, shape, dt=F32):
        return self.ctx.enter_context(self.nc.sbuf_tensor(f"{self.tag}_{name}", shape, dt))

    def ps(self, name, shape):
        return self.ctx.enter_context(self.nc.psum_tensor(f"{self.tag}_{name}", shape, F32))

    def sem(self, name):
        self.sems.append(self.ctx.enter_context(self.nc.semaphore(f"{self.tag}_{name}")))
        return self.sems[-1]

    def block(self):
        return self.nc.Block()


def norm_and_project(nc, d, tag, segments, norm_row, loops, u_tiles=0, u_src=None):
    with Stage(nc, tag) as s:
        hhi = s.sb("hhi", [P, KT, T], F32R)
        hlo = s.sb("hlo", [P, KT, T], F32R)
        ident = s.sb("ident", [P, P])
        gcol = s.sb("gcol", [P, KT])
        xt = [s.sb(f"xt{u}", [P, D]) for u in range(4)]
        hf = [s.sb(f"hf{u}", [P, D]) for u in range(2)]
        sq = s.sb("sq", [P, D])
        ss = [s.sb(f"ss{u}", [P, 4]) for u in range(2)]
        wraw = [s.sb(f"wraw{u}", [P, KT, W256]) for u in range(2)]
        whi = [s.sb(f"whi{u}", [P, KT, W256], F32R) for u in range(2)]
        wlo = [s.sb(f"wlo{u}", [P, KT, W256], F32R) for u in range(2)]
        stage = [s.sb(f"stage{k}", [P, 512]) for k in range(4)]
        if u_tiles:
            us = s.sb("us", [P, 16, CH, GC])
            up = s.sb("up", [NCP, 16, CH, GC])
        tp = [s.ps(f"tp{u}", [P, D]) for u in range(2)]
        ring = [s.ps(f"ring{k}", [P, 512]) for k in range(4)]

        const_in = s.sem("const_in")
        x_in = [s.sem(f"x_in{u}") for u in range(4)]
        x_free = s.sem("x_free")
        sq_done = s.sem("sq_done")
        ms_done = s.sem("ms_done")
        rt_done = s.sem("rt_done")
        rs_done = s.sem("rs_done")
        xn_done = s.sem("xn_done")
        tp_done = s.sem("tp_done")
        hf_done = s.sem("hf_done")
        hi_done = s.sem("hi_done")
        lo_done = s.sem("lo_done")
        w_in = [s.sem(f"w_in{u}") for u in range(2)]
        whi_done = s.sem("whi_done")
        w_ready = s.sem("w_ready")
        w_used = s.sem("w_used")
        grp_done = s.sem("grp_done")
        evac_done = s.sem("evac_done")
        out_done = [s.sem(f"out_done{k}") for k in range(4)]
        u_out = s.sem("u_out")
        waited = s.sem("waited")

        segs, first = [], 0
        for src, n in segments:
            segs.append((src, n, first))
            first += n

        groups_of = {"fm": 6, "fm1": 3, "tm": NT}
        plan, tile0, grp0 = [], u_tiles, u_tiles * 2 * CH
        for n, tiles in loops:
            starts, g = [], 0
            for t in tiles:
                starts.append(g)
                g += groups_of[t[0]]
            plan.append((n, tiles, tile0, grp0, starts, g))
            tile0 += n * len(tiles)
            grp0 += n * g
        n_groups = grp0
        g_first = u_tiles * 2 * CH
        first_widths = [W256, W256] if u_tiles else [x[2] for x in plan[0][1][0:2]]

        with s.block() as block:

            @block.sync
            def _(sp):
                sp.dma_start(ident[:, :], d["ident"][:, :]).then_inc(const_in, 16)
                sp.dma_start(gcol[:, :], norm_row).then_inc(const_in, 16)
                for src, n, f in segs:
                    with sp.Fori(0, n // 4) as i:
                        for u in range(4):
                            sp.wait_ge(x_free, i * 4 + (f + u + 1))
                            sp.dma_start(xt[u][:, :], src[bass.ds(i * (4 * P) + u * P, P), :]).then_inc(x_in[u], 16)
                if u_tiles:
                    with sp.Fori(0, u_tiles // 2) as i:
                        for u in range(2):
                            sp.wait_ge(w_ready, i * 2 + (u + 1))
                            sp.dma_start(wraw[u][:, :, :], u_src(i * (2 * W256) + u * W256, W256)).then_inc(w_in[u], 16)
                for n, tiles, t0, _, _, _ in plan:
                    with sp.Fori(0, n) as i:
                        for j, (kind, src, width, _, _) in enumerate(tiles):
                            sp.wait_ge(w_ready, i * len(tiles) + (t0 + j + 1))
                            sp.dma_start(wraw[j % 2][:, :, 0:width], src(i)).then_inc(w_in[j % 2], 16)

            @block.gpsimd
            def _(pool):
                pool.sem_inc(w_ready, 2)
                for src, n, f in segs:
                    with pool.Fori(0, n // 4) as i:
                        for u in range(4):
                            cols = bass.ds(i * (4 * P) + (f + u) * P, P)
                            pool.wait_ge(hi_done, i * 4 + (f + u + 1))
                            pool.tensor_tensor(hlo[:, :, cols], hf[u % 2][:, :].rearrange("p (k t) -> p k t", k=KT),
                                               hhi[:, :, cols].bitcast(F32), ALU.subtract).then_inc(lo_done, 1)

                def split(u, width, count, tile):
                    pool.wait_ge(w_in[u], count)
                    pool.wait_ge(w_used, tile + 1)
                    pool.sem_inc(waited, 1)
                    pool.tensor_copy(whi[u][:, :, 0:width], wraw[u][:, :, 0:width]).then_inc(whi_done, 1)
                    pool.wait_ge(whi_done, tile + 1)
                    pool.tensor_tensor(wlo[u][:, :, 0:width], wraw[u][:, :, 0:width],
                                       whi[u][:, :, 0:width].bitcast(F32), ALU.subtract).then_inc(w_ready, 1)

                pool.wait_ge(w_ready, 4)
                if u_tiles:
                    with pool.Fori(1, u_tiles // 2) as i:
                        for u in range(2):
                            split(u, W256, i * 16 + 16, i * 2 + u)
                for n, tiles, t0, _, _, _ in plan:
                    with pool.Fori(int(t0 == 0), n) as i:
                        for j, t in enumerate(tiles):
                            split(j % 2, t[2], i * (8 * len(tiles)) + 16 * ((t0 + j) // 2 + 1), i * len(tiles) + t0 + j)

            @block.vector
            def _(dve):
                dve.sem_inc(x_free, 4)
                dve.wait_ge(const_in, 32)
                for src, n, f in segs:
                    with dve.Fori(0, n // 4) as i:
                        for p in (0, 2):
                            for u in (p, p + 1):
                                k = i * 4 + (f + u + 1)
                                st = ss[u % 2]
                                dve.wait_ge(sq_done, k)
                                dve.tensor_scalar(st[:, 1:2], st[:, 0:1], 1.0 / D, EPS, ALU.mult, ALU.add).then_inc(ms_done, 1)
                                dve.wait_ge(rt_done, k)
                                dve.reciprocal(st[:, 3:4], st[:, 2:3]).then_inc(rs_done, 1)
                                dve.wait_ge(rs_done, k)
                                dve.tensor_scalar(xt[u][:, :], xt[u][:, :], st[:, 3:4], None, ALU.mult).then_inc(xn_done, 1)
                            for u in (p, p + 1):
                                k = i * 4 + (f + u + 1)
                                dve.wait_ge(tp_done, k)
                                dve.sem_inc(x_free, 1)
                                dve.wait_ge(lo_done, k)
                                for h in range(2):
                                    dve.tensor_tensor(
                                        hf[u % 2][:, h * 512:(h + 1) * 512].rearrange("p (k t) -> p k t", k=4),
                                        tp[u % 2][:, h * 512:(h + 1) * 512].rearrange("p (k t) -> p k t", k=4),
                                        bc(gcol[:, 4 * h:4 * h + 4], 2, P), ALU.mult).then_inc(hf_done, 1)

                for u, width in enumerate(first_widths):
                    dve.wait_ge(whi_done, u + 1)
                    dve.tensor_tensor(wlo[u][:, :, 0:width], wraw[u][:, :, 0:width],
                                      whi[u][:, :, 0:width].bitcast(F32), ALU.subtract).then_inc(w_ready, 1)

            @block.scalar
            def _(act):
                act.sem_inc(evac_done, 4)
                act.sem_inc(lo_done, 2)
                act.sem_inc(u_out, 32)
                for k in range(4):
                    act.sem_inc(out_done[k], 16)
                for src, n, f in segs:
                    with act.Fori(0, n // 4) as i:
                        for p in (0, 2):
                            for u in (p, p + 1):
                                st = ss[u % 2]
                                act.wait_ge(x_in[u], i * 16 + 16 * (f // 4 + 1))
                                act.activation(sq[:, :], xt[u][:, :], ACT.Square, accum_out=st[:, 0:1]).then_inc(sq_done, 1)
                                act.wait_ge(ms_done, i * 4 + (f + u + 1))
                                act.activation(st[:, 2:3], st[:, 1:2], ACT.Sqrt).then_inc(rt_done, 1)
                            for u in (p, p + 1):
                                act.wait_ge(hf_done, i * 8 + 2 * (f + u + 1))
                                act.activation(hhi[:, :, bass.ds(i * (4 * P) + (f + u) * P, P)],
                                               hf[u % 2][:, :].rearrange("p (k t) -> p k t", k=KT), ACT.Copy).then_inc(hi_done, 1)

                for u, width in enumerate(first_widths):
                    act.wait_ge(w_in[u], 16)
                    act.activation(whi[u][:, :, 0:width], wraw[u][:, :, 0:width], ACT.Copy).then_inc(whi_done, 1)

                if u_tiles:
                    with act.Fori(0, u_tiles // 2) as i:
                        for u in range(2):
                            act.wait_ge(u_out, i * 64 + 32 * (u + 1))
                            for t8 in range(CH):
                                for q, (dst, rows) in enumerate(((us, NCS), (up, NCP))):
                                    g = 2 * CH * u + 2 * t8 + q
                                    act.wait_ge(grp_done, i * (4 * CH) + g + 1)
                                    act.activation(dst[:, :, t8, :],
                                                   ring[g % 4][0:rows, 0:W256].rearrange("p (g c) -> p g c", c=GC),
                                                   ACT.Copy).then_inc(evac_done, 1)
                            act.wait_ge(evac_done, i * (4 * CH) + 2 * CH * (u + 1) + 4)
                            dg = bass.ds(i * 32 + u * 16, 16)
                            act.dma_start(d["u_s"][:, dg, :, :], us[:, :, :, :]).then_inc(u_out, 16)
                            act.dma_start(d["u_p"][:, dg, :, :], up[:, :, :, :]).then_inc(u_out, 16)
                for n, tiles, t0, g0, starts, per in plan:
                    with act.Fori(0, n) as i:
                        for j, (kind, _, width, func, dst) in enumerate(tiles):
                            def store(k):
                                g = g0 + starts[j] + k
                                act.wait_ge(evac_done, i * per + g + 5)
                                if kind != "tm":
                                    out = dst(i, k // 3)[:, (k % 3) * 512:(k % 3 + 1) * 512]
                                    src = stage[g % 4][:, :]
                                else:
                                    out = dst(i, 0)[k * P:(k + 1) * P, :]
                                    src = stage[g % 4][:, 0:width]
                                act.dma_start(out, src).then_inc(out_done[g % 4], 16)

                            for k in range(groups_of[kind]):
                                g = g0 + starts[j] + k
                                act.wait_ge(grp_done, i * per + g + 1)
                                act.wait_ge(out_done[g % 4], i * (4 * per) + 16 * ((g - g_first) // 4 + 1))
                                cols = width if kind == "tm" else 512
                                act.activation(stage[g % 4][:, 0:cols], ring[g % 4][:, 0:cols], func).then_inc(evac_done, 1)
                                if k:
                                    store(k - 1)
                            store(groups_of[kind] - 1)
                for k in range(4):
                    act.wait_ge(out_done[k], 16 * ((n_groups - g_first + 3 - k) // 4 + 1))
                if u_tiles:
                    act.wait_ge(u_out, 32 * (u_tiles + 1))

            @block.tensor
            def _(pe):
                pe.wait_ge(const_in, 32)
                pe.sem_inc(w_used, 2)
                for src, n, f in segs:
                    with pe.Fori(0, n // 4) as i:
                        for u in range(4):
                            pe.wait_ge(xn_done, i * 4 + (f + u + 1))
                            for k in range(KT):
                                mm = pe.transpose(tp[u % 2][:, k * P:(k + 1) * P], xt[u][:, k * P:(k + 1) * P], ident[:, :])
                            mm.then_inc(tp_done, 1)

                def sums(out, lhs, rhs):
                    for k in range(KT):
                        (ah, al), (bh, bl) = lhs(k), rhs(k)
                        pe.matmul(out, ah, bh, start=(k == 0), stop=False)
                        pe.matmul(out, ah, bl, start=False, stop=False)
                        mm = pe.matmul(out, al, bh, start=False, stop=(k == KT - 1))
                    return mm

                pe.wait_ge(lo_done, NT + 2)
                if u_tiles:
                    with pe.Fori(0, u_tiles // 2) as i:
                        for u in range(2):
                            pe.wait_ge(w_ready, i * 2 + (u + 3))
                            for t8 in range(CH):
                                for q, (t0, rows) in enumerate(((LP, NCS), (0, NCP))):
                                    g = 2 * CH * u + 2 * t8 + q
                                    pe.wait_ge(evac_done, i * (4 * CH) + g + 1)
                                    sel = slice(t0 + t8, t0 + t8 + CH * (rows - 1) + 1, CH)
                                    sums(ring[g % 4][0:rows, 0:W256],
                                         lambda k: (hhi[:, k, sel], hlo[:, k, sel]),
                                         lambda k: (whi[u][:, k, :], wlo[u][:, k, :])).then_inc(grp_done, 1)
                            pe.wait_ge(grp_done, i * (4 * CH) + 2 * CH * (u + 1))
                            pe.sem_inc(w_used, 1)
                for n, tiles, t0, g0, starts, per in plan:
                    with pe.Fori(0, n) as i:
                        for j, (kind, _, width, func, dst) in enumerate(tiles):
                            u = j % 2
                            pe.wait_ge(w_ready, i * len(tiles) + (t0 + j + 3))
                            for k in range(groups_of[kind]):
                                g = g0 + starts[j] + k
                                pe.wait_ge(evac_done, i * per + g + 1)
                                if kind != "tm":
                                    h, c = divmod(k, 3)
                                    wc, tc = slice(h * P, (h + 1) * P), slice(c * 512, (c + 1) * 512)
                                    mm = sums(ring[g % 4][:, :],
                                              lambda k: (whi[u][:, k, wc], wlo[u][:, k, wc]),
                                              lambda k: (hhi[:, k, tc], hlo[:, k, tc]))
                                else:
                                    tc = slice(k * P, (k + 1) * P)
                                    mm = sums(ring[g % 4][:, 0:width],
                                              lambda k: (hhi[:, k, tc], hlo[:, k, tc]),
                                              lambda k: (whi[u][:, k, 0:width], wlo[u][:, k, 0:width]))
                                mm.then_inc(grp_done, 1)
                            pe.wait_ge(grp_done, i * per + g + 1)
                            pe.sem_inc(w_used, 1)


def even_input_projection(nc, d):
    w = d["e_w_in"].rearrange("(k p) n -> p k n", p=P)
    norm_and_project(
        nc, d, "ei", ((d["x_prompt"], LP // P), (d["x_sample"], LS // P)), d["pre_col"][0],
        (
            (D // W256, (
                ("fm", lambda i: w[:, :, bass.ds(i * W256 + E_ZA, W256)], W256, ACT.Silu,
                 lambda i, h: d["za"][bass.ds(i * W256 + h * P, P), :]),
                ("fm", lambda i: w[:, :, bass.ds(i * W256 + E_ZB, W256)], W256, ACT.Silu,
                 lambda i, h: d["zb"][bass.ds(i * W256 + h * P, P), :]),
            )),
            (2, tuple(
                ("tm", lambda i, a=a: w[:, :, bass.ds(i * 352 + a + E_CQ, 176)], 176, ACT.Copy,
                 lambda i, h, a=a: d["cq"][:, bass.ds(i * 352 + a, 176)]) for a in (0, 176))),
        ),
        u_tiles=D // W256, u_src=lambda c, n: w[:, :, bass.ds(c + E_U, n)])


def s5(nc, d):
    NB, GP = 8, 4
    NPAIR = G5 // 2
    Q = 2 * NPAIR
    TC = CH * GC
    NC = NCS + NCP
    TWO_PI = 2 * math.pi
    C1 = 6.28125
    C2 = round((TWO_PI - C1) * 2 ** 21) / 2 ** 21
    C3 = TWO_PI - C1 - C2
    MAGIC = 1.5 * 2 ** 23

    with Stage(nc, "sa") as s:
        pw = [s.sb(f"pw{x}", [P, CH + 1, 2, NPAIR]) for x in "ri"]
        pwd = [s.sb(f"pwd{x}", [P, CH + 1, 2, NPAIR]) for x in "ri"]
        bb = [s.sb(f"bb{x}", [P, 2, NPAIR, GC]) for x in "ri"]
        b0 = [s.sb(f"b0{x}", [P, 2, NPAIR, GC]) for x in "ri"]
        cc = [s.sb(f"cc{x}", [P, 2, NPAIR, GC]) for x in "ri"]
        nc_ = [s.sb(f"nc{x}", [P, 2, NPAIR, GC]) for x in "ri"]
        small = s.sb("small", [P, 16, Q])
        pt = [s.sb(f"pt{k}", [P, 4, Q]) for k in range(4)]
        ua = [s.sb(f"ua{x}", [P, 2 * CH, 2, NPAIR]) for x in "ri"]
        ub = [s.sb(f"ub{x}", [P, CH + 1, 2, NPAIR]) for x in "ri"]
        un = [s.sb(f"un{x}", [P, Q]) for x in "ri"]
        turns = [[s.sb(f"turn{u}{x}", [P, 2, GP, NC]) for x in "cs"] for u in range(2)]
        pt2 = [s.sb(f"pt2{k}", [P, 4, Q]) for k in range(4)]
        rho = s.sb("rho", [P, 2, GP, NC])
        zz = [s.sb(f"zz{x}", [P, 2, GP, NC]) for x in "ri"]
        vp = [s.sb(f"vp{j}", [P, 2, 2, NC]) for j in range(GP)]
        rt_ = [s.sb(f"rt{k}", [P, 2, NC]) for k in range(4)]
        po = [s.sb(f"po{k}", [P, 2, GP, NC]) for k in range(2)]
        hs = s.sb("hs", [P, 2, 2, GP, NC])
        bp = s.sb("bp", [P, 2, 2, GP, TC])
        cp = s.sb("cp", [P, 2, 2, GP, (CH + 1) * GC])
        bt_ = [s.sb(f"bt{k}", [P, GP, CH, GC]) for k in range(4)]
        ct_ = [s.sb(f"ct{k}", [P, GP, CH + 1, GC]) for k in range(4)]
        us = s.sb("us", [P, 2 * GP, TC])
        up = s.sb("up", [NCP, 2 * GP, TC])
        btr = [s.sb(f"btr{u}", [P, 2, 2, P]) for u in range(2)]
        ut = [s.sb(f"ut{u}", [P, 2, NC]) for u in range(2)]
        rows = s.sb("rows", [GC, 2 * GP, 15, GC])
        dd = s.sb("dd", [GC, 2 * GP, GC])
        dsk = s.sb("dsk", [GC, G5])
        ident = s.sb("ident", [P, P])
        pb = [s.ps(f"pb{u}", [P, 512]) for u in range(2)]
        pu = [s.ps(f"pu{u}", [P, 512]) for u in range(2)]
        pv = s.ps("pv", [P, 2, 512])
        pk = [s.ps(f"pk{g}", [P, 512]) for g in range(2)]
        const_in, chain, sin_in, sin_out, tab_done = (s.sem(x) for x in ("const_in", "chain", "sin_in", "sin_out", "tab_done"))
        neg_done = s.sem("neg_done")
        bp_mul, bp_done, cp_mul, cp_done, bt_mm, bt_done, ut_mm, ut_done = (
            s.sem(x) for x in ("bp_mul", "bp_done", "cp_mul", "cp_done", "bt_mm", "bt_done", "ut_mm", "ut_done"))
        v_mm, v_done, k_mm, k_done, dd_done, row_done = (
            s.sem(x) for x in ("v_mm", "v_done", "k_mm", "k_done", "dd_done", "row_done"))
        u_in, cp_out, row_out, waited = (s.sem(x) for x in ("u_in", "cp_out", "row_out", "waited"))
        ut_out = [s.sem(f"ut_out{u}") for u in range(2)]
        z_set, links2, ph_done, t_mul, t_add, rot_mul, rot_done, rho_done, scan_done, pm_done, hs_done, hs_out = (
            s.sem(x) for x in ("z_set", "links2", "ph_done", "t_mul", "t_add", "rot_mul", "rot_done", "rho_done", "scan_done", "pm_done",
                               "hs_done", "hs_out"))

        with s.block() as block:

            @block.sync
            def _(sp):
                for dst, src in ((small[:, 0, :].rearrange("p (a b) -> p a b", a=2), d["lam_re"]), (small[:, 1, :].rearrange("p (a b) -> p a b", a=2), d["lam_im"]),
                                 (small[:, 2, :].rearrange("p (a b) -> p a b", a=2), d["log_dt"]), (b0[0][:, :, :, :], d["b_re"]), (b0[1][:, :, :, :], d["b_im"]),
                                 (cc[0][:, :, :, :], d["c_re"]), (cc[1][:, :, :, :], d["c_im"]), (dsk[:, :], d["d_skip"]),
                                 (ident[:, :], d["ident"])):
                    sp.dma_start(dst, src).then_inc(const_in, 16)
                def batch(b):
                    sp.wait_ge(ut_mm, b * (2 * GP) + 1)
                    sp.dma_start(us[:, :, :], d["u_s"][:, bass.ds(b * (2 * GP), 2 * GP), :, :].rearrange("n g t c -> n g (t c)")).then_inc(u_in, 16)
                    sp.dma_start(up[:, :, :], d["u_p"][:, bass.ds(b * (2 * GP), 2 * GP), :, :].rearrange("n g t c -> n g (t c)")).then_inc(u_in, 16)
                    for j in range(GP):
                        sp.wait_ge(ut_done, b * GP + j + 1)
                        sp.dma_start(d["utd"][bass.ds(b * GP + j, 1), :, :].rearrange("a p n -> p (a n)"),
                                     ut[j % 2][:, :, :].rearrange("p g n -> p (g n)")).then_inc(ut_out[j % 2], 16)
                    sp.wait_ge(cp_done, b * 4 + 4)
                    sp.dma_start(d["cpow"][bass.ds(b, 1), :, :].rearrange("a p n -> p (a n)"),
                                 cp[:, :, :, :, :].rearrange("p d r g n -> p (d r g n)")).then_inc(cp_out, 16)
                    sp.wait_ge(row_done, b + 2)
                    sp.dma_start(d["lagrow"][bass.ds(b * (2 * GP), 2 * GP), :, :].rearrange("g c n -> c g n"),
                                 rows[:, :, :, :].rearrange("c g l n -> c g (l n)")).then_inc(row_out, 16)

                def states(b):
                    sp.wait_ge(hs_done, b * 8 + 9)
                    sp.sem_inc(waited, 1)
                    sp.dma_start(d["hst"][bass.ds(b, 1), :, :].rearrange("a p n -> p (a n)"),
                                 hs[:, :, :, :, :].rearrange("p d r g n -> p (d r g n)")).then_inc(hs_out, 16)

                batch(0)
                with sp.Fori(0, NB - 1) as b:
                    batch(b + 1)
                    states(b)
                states(NB - 1)
                sp.wait_ge(hs_out, 16 * (NB + 1))
                for u in range(2):
                    sp.wait_ge(ut_out[u], 16 * (NPAIR // 2 + 1))
                sp.wait_ge(cp_out, 16 * (NB + 1))
                sp.wait_ge(row_out, 16 * (NB + 1))

            @block.scalar
            def _(act):
                for u in range(2):
                    act.sem_inc(ut_out[u], 16)
                act.sem_inc(cp_out, 16)
                act.sem_inc(rot_done, 8)
                act.sem_inc(hs_out, 16)
                act.sem_inc(row_out, 16)
                act.wait_ge(const_in, 144)
                act.activation(small[:, 3, :], small[:, 2, :], ACT.Exp).then_inc(sin_out, 1)
                act.wait_ge(sin_in, 1)
                act.activation(small[:, 6, :], small[:, 4, :], ACT.Exp).then_inc(sin_out, 1)
                act.wait_ge(sin_in, 2)
                act.activation(small[:, 9, :], small[:, 7, :], ACT.Sin).then_inc(sin_out, 1)
                act.activation(small[:, 10, :], small[:, 8, :], ACT.Sin).then_inc(sin_out, 1)
                for x in range(2):
                    act.mul(nc_[x][:, :, :, :], cc[x][:, :, :, :], -1.0).then_inc(neg_done, 1)
                with act.Fori(0, NB) as b:
                    for j in range(GP):
                        n = b * GP + j
                        act.wait_ge(bt_mm, n + 1)
                        act.wait_ge(v_mm, b * GP + j + 1)
                        act.activation(btr[j % 2][:, :, :, :].rearrange("p a b c -> p (a b c)"), pb[j % 2][:, :], ACT.Copy).then_inc(bt_done, 1)
                        act.wait_ge(ut_mm, b * (2 * GP) + 2 * j + 3)
                        act.wait_ge(ut_out[j % 2], b * (8 * GP) + 16 * (j // 2 + 1))
                        act.activation(ut[j % 2][:, :, :].rearrange("p g n -> p (g n)"), pu[j % 2][:, 0:2 * NC], ACT.Copy).then_inc(ut_done, 1)
                        act.wait_ge(v_mm, n + 3)
                        act.wait_ge(rot_done, b * (2 * GP) + 2 * j + 2)
                        act.sem_inc(waited, 1)
                        for dr, to, at in ((0, slice(0, NC), slice(0, NC)), (1, slice(0, NCS), slice(NCS - 1, None, -1)),
                                           (1, slice(NCS, NC), slice(NC - 1, NCS - 1, -1))):
                            act.activation(vp[j][:, dr, :, to], pv[:, dr, 0:2 * NC].rearrange("p (r n) -> p r n", r=2)[:, :, at],
                                           ACT.Copy).then_inc(v_done, 1)
                    act.wait_ge(scan_done, b * 2 + 2)
                    act.wait_ge(ph_done, 1)
                    act.sem_inc(waited, 1)
                    for lo, hi in ((1, NCS), (NCS + 1, NC)):
                        src = bc(small[:, 15, :].rearrange("p (a g) -> p a g", a=2)[:, :, bass.ds(b * GP, GP)], 3, hi - lo)
                        act.activation(rho[:, :, :, lo:hi], src, ACT.Copy).then_inc(rho_done, 1)

            @block.vector
            def _(dve):
                links = [0]

                def link(ins):
                    links[0] += 1
                    ins.then_inc(chain, 1)
                    dve.wait_ge(chain, links[0])

                def sm(k):
                    return small[:, k, :]

                tt = dve.tensor_tensor
                dve.wait_ge(const_in, 144)
                link(dve.tensor_scalar(sm(0), sm(0), -1e-4, None, ALU.min))
                dve.wait_ge(sin_out, 1)
                link(tt(sm(4), sm(0), sm(3), ALU.mult))
                dve.sem_inc(sin_in, 1)
                link(tt(sm(5), sm(1), sm(3), ALU.mult))
                link(dve.tensor_scalar(sm(11), sm(5), 1.0 / TWO_PI, MAGIC, ALU.mult, ALU.add))
                link(dve.tensor_scalar(sm(11), sm(11), MAGIC, None, ALU.subtract))
                for c in (C1, C2, C3):
                    link(dve.scalar_tensor_tensor(sm(5), sm(11), -c, sm(5), ALU.mult, ALU.add))
                link(dve.tensor_scalar(sm(7), sm(5), 3.1415925, -3.1415925, ALU.min, ALU.max))
                link(dve.tensor_scalar(sm(8), sm(7), -1.0, None, ALU.mult))
                link(tt(sm(8), sm(8), sm(7), ALU.max))
                link(dve.tensor_scalar(sm(8), sm(8), -1.0, math.pi / 2, ALU.mult, ALU.add))
                dve.sem_inc(sin_in, 1)
                dve.wait_ge(sin_out, 4)

                def pwk(x, a, b):
                    return pw[x][:, a:b, :, :].rearrange("p k d g -> p k (d g)")

                link(dve.memset(pwk(0, 0, 1), 1.0))
                link(dve.memset(pwk(1, 0, 1), 0.0))
                link(tt(pwk(0, 1, 2), small[:, 6:7, :], small[:, 10:11, :], ALU.mult))
                link(tt(pwk(1, 1, 2), small[:, 6:7, :], small[:, 9:10, :], ALU.mult))

                def cmul(out, a, b, t):
                    link(tt(t[0], a[0], b[0], ALU.mult))
                    link(tt(t[1], a[1], b[1], ALU.mult))
                    link(tt(t[2], a[0], b[1], ALU.mult))
                    link(tt(t[3], a[1], b[0], ALU.mult))
                    link(tt(out[0], t[0], t[1], ALU.subtract))
                    link(tt(out[1], t[2], t[3], ALU.add))

                for n in (1, 2, 4):
                    cmul([pwk(x, n + 1, 2 * n + 1) for x in range(2)], [pwk(x, 1, n + 1) for x in range(2)],
                         [pwk(x, n, n + 1).broadcast_to([P, n, Q]) for x in range(2)], [t[:, 0:n, :] for t in pt])
                for x in range(2):
                    for k in range(CH + 1):
                        link(dve.tensor_copy(pwd[x][:, k, :, :], pw[x][:, CH - k, :, :]))
                lr, li, nr, ni = sm(0), sm(1), sm(12), pw[1][:, 1, :, :].rearrange("p d g -> p (d g)")
                link(dve.tensor_scalar(nr, pw[0][:, 1, :, :].rearrange("p d g -> p (d g)"), 1.0, None, ALU.subtract))
                link(tt(sm(2), lr, lr, ALU.mult))
                link(tt(sm(3), li, li, ALU.mult))
                link(tt(sm(2), sm(2), sm(3), ALU.add))
                link(dve.reciprocal(sm(3), sm(2)))
                for a, x, y, op in ((13, (nr, lr), (ni, li), ALU.add), (14, (ni, lr), (nr, li), ALU.subtract)):
                    link(tt(sm(4), x[0], x[1], ALU.mult))
                    link(tt(sm(5), y[0], y[1], ALU.mult))
                    link(tt(sm(4), sm(4), sm(5), op))
                    link(tt(sm(a), sm(4), sm(3), ALU.mult))
                cf = [bc(sm(a), 2, GC) for a in (13, 14)]
                fl = [[x[:, :, :, :].rearrange("p d g c -> p (d g) c") for x in y] for y in (b0, bb)]
                tmp = [bp[:, x // 2, x % 2, :, :].rearrange("p g n -> p (g n)").rearrange("p (q c) -> p q c", c=GC) for x in range(4)]
                for h in range(2):
                    sl = slice(32 * h, 32 * h + 32)
                    cmul([f[:, sl, :] for f in fl[1]], [f[:, sl, :] for f in fl[0]], [c[:, sl, :] for c in cf], tmp)
                dve.sem_inc(tab_done, 1)
                base = links[0]
                def scan(b):
                    dve.wait_ge(rho_done, b * 2 + 2)
                    dve.wait_ge(rot_done, b * (2 * GP) + 2 * GP)
                    for x in zz:
                        row = x[:, :, :, :].rearrange("p d g n -> p (d g n)")
                        dve.tensor_tensor_scan(row, rho[:, :, :, :].rearrange("p d g n -> p (d g n)"), row, 0.0, ALU.mult,
                                               ALU.add).then_inc(scan_done, 1)

                def turn(b, u):
                    dve.wait_ge(pm_done, b * 4 + 4)
                    dve.sem_inc(waited, 1)
                    for k, (pairs, op) in enumerate(((((0, 0), (1, 1)), ALU.subtract), (((0, 1), (1, 0)), ALU.add))):
                        dve.wait_ge(t_add, b * 4 + 2 * k + 4)
                        dve.sem_inc(waited, 1)
                        for m, (x, y) in enumerate(pairs):
                            for dr in range(2):
                                dve.tensor_tensor(b0[m][:, dr, :, :].rearrange("p g c -> p (g c)").rearrange(
                                    "p (j a c) -> p j a c", j=GP, a=2 * CH),
                                    bc(ua[x][:, :, dr, bass.ds(b * GP, GP)].rearrange("p k g -> p g k"), 3, CH),
                                    bc(ub[y][:, 0:CH, dr, bass.ds(b * GP, GP)].rearrange("p k g -> p g k"), 2, 2 * CH),
                                    ALU.mult).then_inc(t_mul, 1)
                        dve.wait_ge(t_mul, b * 8 + 4 * k + 4)
                        m0, m1 = (x[:, :, :, :].rearrange("p a g c -> p (a g c)").rearrange("p (d j n) -> p d j n", d=2, j=GP) for x in b0)
                        dve.tensor_tensor(turns[u][k][:, :, :, 0:NCS], m0, m1, op).then_inc(t_add, 1)
                        dve.wait_ge(t_add, b * 4 + 2 * k + 5)
                        dve.tensor_copy(turns[u][k][:, :, :, NCS:NC], turns[u][k][:, :, :, 0:NCP]).then_inc(t_add, 1)

                def rotate(b, u, j):
                    c, sn = (x[:, :, j, :] for x in turns[u])
                    vr, vi = vp[j][:, :, 0, :], vp[j][:, :, 1, :]
                    dve.wait_ge(v_done, b * (3 * GP) + 3 * j + 4)
                    dve.wait_ge(t_add, b * 4 + 8)
                    dve.wait_ge(pm_done, b * 4 + 8)
                    dve.wait_ge(rot_done, b * (2 * GP) + 2 * j + 8)
                    for k, (x, y) in enumerate(((vr, c), (vi, sn), (vi, c), (vr, sn))):
                        dve.tensor_tensor(rt_[k][:, :, :], x, y, ALU.mult).then_inc(rot_mul, 1)
                    dve.wait_ge(rot_mul, b * (4 * GP) + 4 * j + 4)
                    dve.tensor_tensor(zz[0][:, :, j, :], rt_[0][:, :, :], rt_[1][:, :, :], ALU.add).then_inc(rot_done, 1)
                    dve.tensor_tensor(zz[1][:, :, j, :], rt_[2][:, :, :], rt_[3][:, :, :], ALU.subtract).then_inc(rot_done, 1)

                dve.wait_ge(z_set, 2)
                dve.wait_ge(ph_done, 1)

                def batch(b, u):
                    gp = bass.ds(b * GP, GP)
                    dve.wait_ge(k_mm, b * GP + 1)
                    dve.sem_inc(waited, 1)
                    for dr in range(2):
                        if dr:
                            dve.wait_ge(bp_done, b * 4 + 6)
                            dve.sem_inc(waited, 1)
                        else:
                            dve.wait_ge(bp_done, b * 4 + 4)
                            dve.sem_inc(waited, 1)
                        src = [x[:, 1:CH + 1, dr, gp] for x in pwd] if dr == 0 else [x[:, 0:CH, dr, gp] for x in pw]
                        pk_ = [bc(src[x].rearrange("p k g -> p g k"), 3, GC) for x in range(2)]
                        bk_ = [bc(bb[x][:, dr, gp, :], 2, CH) for x in range(2)]
                        for t, (x, y) in enumerate(((0, 0), (1, 1), (0, 1), (1, 0))):
                            dve.tensor_tensor(bt_[t][:, :, :, :], pk_[x], bk_[y], ALU.mult).then_inc(bp_mul, 1)
                        dve.wait_ge(bp_mul, b * 8 + 4 * (dr + 1))
                        for r, op in ((0, ALU.subtract), (1, ALU.add)):
                            dve.tensor_tensor(bp[:, dr, r, :, :].rearrange("p g n -> p (g n)"),
                                              bt_[2 * r][:, :, :, :].rearrange("p g t c -> p (g t c)"),
                                              bt_[2 * r + 1][:, :, :, :].rearrange("p g t c -> p (g t c)"), op).then_inc(bp_done, 1)
                    dve.wait_ge(row_done, b + 1)
                    dve.tensor_tensor(dd[:, :, :], bc(ident[0:GC, 0:GC], 1, 2 * GP), bc(dsk[:, bass.ds(b * (2 * GP), 2 * GP)], 2, GC),
                                      ALU.mult).then_inc(dd_done, 1)
                    for j in range(GP):
                        if j == 0:
                            scan(b)
                        dve.wait_ge(k_mm, b * GP + j + 2)
                        if j == 0:
                            dve.wait_ge(row_out, b * 16 + 16)
                        to = [rows[:, 2 * j + g, :, :].rearrange("c l n -> c (l n)") for g in range(2)]
                        for g in range(2):
                            dve.tensor_copy(to[g][:, 0:TC], pk[g][0:GC, TC:2 * TC]).then_inc(k_done, 1)
                            dve.tensor_copy(to[g][:, TC:15 * GC], pk[g][0:GC, GC:TC]).then_inc(k_done, 1)
                        dve.wait_ge(k_done, b * (6 * GP) + 6 * j + 5)
                        for g in range(2):
                            dve.tensor_tensor(to[g][:, 7 * GC:TC], to[g][:, 7 * GC:TC], pk[g][0:GC, 0:GC], ALU.add).then_inc(k_done, 1)
                        if j == 0:
                            turn(b, u)
                        else:
                            rotate(b, u, j - 1)
                    dve.wait_ge(k_done, b * (6 * GP) + (6 * GP + 1))
                    dve.wait_ge(dd_done, b + 1)
                    dve.tensor_tensor(rows[:, :, 7, :], rows[:, :, 7, :], dd[:, :, :], ALU.add).then_inc(row_done, 1)
                    rotate(b, u, GP - 1)

                with dve.Fori(0, NB // 2) as i:
                    for u in range(2):
                        batch(i * 2 + u, u)
                scan(NB)

            @block.gpsimd
            def _(pool):
                pool.sem_inc(pm_done, 8)
                for x in zz:
                    pool.memset(x[:, :, :, :], 0.0).then_inc(z_set, 1)
                for dr in range(2):
                    pool.memset(rho[:, dr, :, :], 0.0).then_inc(rho_done, 1)
                for dr, cols in ((0, (0, NCS)), (1, (NCS - 1, NC - 1))):
                    for c in cols:
                        pool.memset(hs[:, dr, :, :, c:c + 1], 0.0).then_inc(z_set, 1)
                pool.wait_ge(z_set, 6)
                pool.sem_inc(hs_done, 1)
                links = [0]

                def link(ins):
                    links[0] += 1
                    ins.then_inc(links2, 1)
                    pool.wait_ge(links2, links[0])

                def sm(k):
                    return small[:, k, :]

                ptt = pool.tensor_tensor

                def cmul2(out, a, b, t):
                    link(ptt(t[0], a[0], b[0], ALU.mult))
                    link(ptt(t[1], a[1], b[1], ALU.mult))
                    link(ptt(t[2], a[0], b[1], ALU.mult))
                    link(ptt(t[3], a[1], b[0], ALU.mult))
                    link(ptt(out[0], t[0], t[1], ALU.subtract))
                    link(ptt(out[1], t[2], t[3], ALU.add))

                pool.wait_ge(sin_out, 4)
                link(ptt(sm(15), sm(6), sm(6), ALU.mult))
                for _ in range(2):
                    link(ptt(sm(15), sm(15), sm(15), ALU.mult))
                unk = [x[:, :].unsqueeze(1) for x in un]
                t1 = [t[:, 0:1, :] for t in pt2]
                cmul2(unk, [small[:, k:k + 1, :] for k in (10, 9)], [small[:, k:k + 1, :] for k in (10, 9)], t1)
                cmul2(unk, unk, unk, t1)

                def uk(x, a, b):
                    return x[:, a:b, :, :].rearrange("p k d g -> p k (d g)")

                cmul2([uk(x, 1, 2) for x in ub], unk, unk, t1)
                for tab, ns in ((ub, (1, 2, 4)), (ua, (1, 2, 4, 8))):
                    if tab is ua:
                        for x in range(2):
                            link(pool.tensor_copy(uk(ua[x], 1, 2), uk(ub[x], CH, CH + 1)))
                    link(pool.memset(uk(tab[0], 0, 1), 1.0))
                    link(pool.memset(uk(tab[1], 0, 1), 0.0))
                    for n in ns:
                        for lo in range(0, n, 4):
                            w = min(4, n - lo, tab[0].shape[1] - 1 - n - lo)
                            cmul2([uk(x, n + 1 + lo, n + 1 + lo + w) for x in tab], [uk(x, 1 + lo, 1 + lo + w) for x in tab],
                                 [uk(x, n, n + 1).broadcast_to([P, w, Q]) for x in tab], [t[:, 0:w, :] for t in pt2])
                pool.sem_inc(ph_done, 1)
                pool.wait_ge(tab_done, 1)
                pool.wait_ge(neg_done, 2)
                def powers(b):
                    gp = bass.ds(b * GP, GP)
                    pool.wait_ge(k_mm, b * GP + 1)
                    pool.wait_ge(cp_out, b * 16 + 16)
                    pool.sem_inc(waited, 1)
                    for dr in range(2):
                        pool.wait_ge(cp_done, b * 4 + 2 * dr) if dr else pool.wait_ge(cp_mul, b * 8 + 1)
                        pool.sem_inc(waited, 1)
                        pk_ = [bc((pwd if dr else pw)[x][:, :, dr, gp].rearrange("p k g -> p g k"), 3, GC) for x in range(2)]
                        src = [bc(c[:, dr, gp, :], 2, CH + 1) for c in (cc[0], nc_[1], nc_[0], nc_[1])]
                        for t, x in enumerate((0, 1, 1, 0)):
                            pool.tensor_tensor(ct_[t][:, :, :, :], pk_[x], src[t], ALU.mult).then_inc(cp_mul, 1)
                        pool.wait_ge(cp_mul, b * 8 + (4 * (dr + 1) + 1))
                        for r in range(2):
                            pool.tensor_tensor(cp[:, dr, r, :, :].rearrange("p g n -> p (g n)"),
                                               ct_[2 * r][:, :, :, :].rearrange("p g t c -> p (g t c)"),
                                               ct_[2 * r + 1][:, :, :, :].rearrange("p g t c -> p (g t c)"), ALU.add).then_inc(cp_done, 1)
                    pool.wait_ge(cp_done, b * 4 + 4)

                def states(b, u):
                    pool.wait_ge(scan_done, b * 2 + 4)
                    pool.wait_ge(hs_out, b * 16 + 16)
                    c, sn = turns[u]
                    for r, (x, y, op) in enumerate(((c, sn, ALU.subtract), (sn, c, ALU.add))):
                        pool.wait_ge(hs_done, b * 8 + 4 * r + 1)
                        for k, (a, t) in enumerate(((zz[0], x), (zz[1], y))):
                            pool.tensor_tensor(po[k][:, :, :, :].rearrange("p d g n -> p (d g n)"),
                                               a[:, :, :, :].rearrange("p d g n -> p (d g n)"),
                                               t[:, :, :, :].rearrange("p d g n -> p (d g n)"), ALU.mult).then_inc(pm_done, 1)
                        pool.wait_ge(pm_done, b * 4 + 2 * r + 10)
                        for dr, to, at in ((0, slice(1, NCS), slice(0, NCS - 1)), (0, slice(NCS + 1, NC), slice(NCS, NC - 1)),
                                           (1, slice(0, NCS - 1), slice(NCS - 2, None, -1)),
                                           (1, slice(NCS, NC - 1), slice(NC - 2, NCS - 1, -1))):
                            pool.tensor_tensor(hs[:, dr, r, :, to], po[0][:, dr, :, at], po[1][:, dr, :, at], op).then_inc(hs_done, 1)

                powers(0)
                with pool.Fori(0, NB // 2 - 1) as i:
                    for u in range(2):
                        powers(i * 2 + (u + 1))
                        states(i * 2 + u, u)
                powers(NB - 1)
                states(NB - 2, 0)
                states(NB - 1, 1)

            @block.tensor
            def _(pe):
                pe.sem_inc(ut_mm, 1)
                pe.sem_inc(v_mm, 2)
                pe.sem_inc(k_mm, 1)
                pe.sem_inc(bp_done, 4)
                pe.sem_inc(cp_mul, 1)
                pe.sem_inc(k_done, 1)
                pe.sem_inc(v_done, 1)
                pe.sem_inc(row_done, 1)
                pe.sem_inc(t_add, 4)
                pe.wait_ge(const_in, 144)
                pe.wait_ge(tab_done, 1)
                with pe.Fori(0, NB) as b:
                    pe.wait_ge(bp_done, b * 4 + 8)
                    pe.wait_ge(u_in, b * 32 + 32)
                    for j in range(GP):
                        for x in range(4):
                            mm = pe.transpose(pb[j % 2][:, x * P:(x + 1) * P], bp[:, x // 2, x % 2, j, :], ident[:, :])
                        mm.then_inc(bt_mm, 1)
                        for g in range(2):
                            pe.transpose(pu[j % 2][:, g * NC:g * NC + NCS], us[:, 2 * j + g, :], ident[:, :])
                            pe.transpose(pu[j % 2][:, g * NC + NCS:(g + 1) * NC], up[:, 2 * j + g, :],
                                         ident[0:NCP, 0:NCP]).then_inc(ut_mm, 1)
                        pe.wait_ge(bt_done, b * GP + j + 1)
                        pe.wait_ge(ut_done, b * GP + j + 1)
                        pe.wait_ge(v_done, b * (3 * GP) + 3 * j + 1)
                        pe.sem_inc(waited, 1)
                        for g in range(2):
                            for x in range(4):
                                r = x % 2
                                mm = pe.matmul(pv[64 * g:64 * g + 64, x // 2, r * NC:(r + 1) * NC],
                                               btr[j % 2][:, x // 2, r, 64 * g:64 * g + 64], ut[j % 2][:, g, :], start=True, stop=True,
                                               skip_group_check=True)
                        mm.then_inc(v_mm, 1)
                        if j == 0:
                            pe.wait_ge(cp_done, b * 4 + 4)
                        pe.wait_ge(k_done, b * (6 * GP) + 6 * j + 1)
                        pe.sem_inc(waited, 1)
                        for g in range(2):
                            h = slice(64 * g, 64 * g + 64)
                            for dr in range(2):
                                at = (7 * GC, 0)[dr]
                                for r in range(2):
                                    mm = pe.matmul(pk[g][0:GC, dr * TC:(dr + 1) * TC],
                                                   bp[h, dr, r, j, at:at + GC], cp[h, dr, r, j, dr * GC:dr * GC + TC],
                                                   start=(r == 0), stop=(r == 1), skip_group_check=True)
                        mm.then_inc(k_mm, 1)

    with Stage(nc, "sy") as s:
        cp = [s.sb(f"cp{u}", [P, 2, 2, GP, (CH + 1) * GC]) for u in range(2)]
        wt = [s.sb(f"wt{u}", [P, 2 * GP, TC]) for u in range(2)]
        ut = [s.sb(f"ut{u}", [P, GP, 2 * NC]) for u in range(2)]
        hs = [s.sb(f"hs{u}", [P, 2, 2, GP, NC]) for u in range(2)]
        ys = s.sb("ys", [P, CH, 2 * GP, GC])
        yp = s.sb("yp", [NCP, CH, 2 * GP, GC])
        go = s.sb("go", [P, T])
        ident = s.sb("ident", [P, P])
        py = [s.ps(f"py{k}", [P, 512]) for k in range(4)]
        pt = [s.ps(f"pt{k}", [P, 512]) for k in range(3)]
        const_in, y_mm, g_done, t_mm, go_done, go_out, waited = (
            s.sem(x) for x in ("const_in", "y_mm", "g_done", "t_mm", "go_done", "go_out", "waited"))
        t_in = [s.sem(f"t_in{u}") for u in range(2)]
        with s.block() as block:

            @block.sync
            def _(sp):
                sp.dma_start(ident[:, :], d["ident"][:, :]).then_inc(const_in, 16)
                with sp.Fori(0, NB // 2) as i:
                    for u in range(2):
                        sp.wait_ge(y_mm, i * 8 + 4 * u + 4)
                        sp.dma_start(cp[u][:, :, :, :, :].rearrange("p d r g n -> p (d r g n)"),
                                     d["cpow"][bass.ds(i * 2 + u, 1), :, :].rearrange("a p n -> p (a n)")).then_inc(t_in[u], 16)
                        sp.dma_start(ut[u][:, :, :], d["utd"][bass.ds(i * (2 * GP) + u * GP, GP), :, :].rearrange("g p n -> p g n")).then_inc(t_in[u], 16)
                        sp.dma_start(hs[u][:, :, :, :, :].rearrange("p d r g n -> p (d r g n)"),
                                     d["hst"][bass.ds(i * 2 + u, 1), :, :].rearrange("a p n -> p (a n)")).then_inc(t_in[u], 16)
                        for t in range(CH):
                            at = (CH - 1 - t) * GC
                            sp.dma_start(wt[u][t * GC:(t + 1) * GC, :, :],
                                         d["lagrow"][bass.ds(i * (4 * GP) + u * 2 * GP, 2 * GP), :, at:at + TC].rearrange("g c n -> c g n")
                                         ).then_inc(t_in[u], 16)

            @block.scalar
            def _(act):
                act.sem_inc(go_out, 16)
                with act.Fori(0, NB) as b:
                    for k in range(4):
                        act.wait_ge(y_mm, b * 4 + (k + 9))
                        act.wait_ge(t_mm, b * 3 + 3)
                        rows = NCS if k < 2 else NCP
                        h = k % 2
                        out = (ys if k < 2 else yp)[:, :, h::2, :].rearrange("p t g c -> p g t c")
                        act.activation(out, py[k][0:rows, :].rearrange("p (g t c) -> p g t c", g=4, t=CH),
                                       ACT.Gelu_apprx_tanh).then_inc(g_done, 1)
                    act.wait_ge(go_done, b * 3 + 3)
                    act.dma_start(d["gt"][bass.ds(b * P, P), :], go[:, :]).then_inc(go_out, 16)
                act.wait_ge(go_out, 16 * (NB + 1))

            @block.vector
            def _(dve):
                with dve.Fori(0, NB) as b:
                    for k in range(3):
                        dve.wait_ge(t_mm, b * 3 + (k + 4))
                        dve.wait_ge(go_out, b * 16 + 16)
                        if k < 2:
                            out = go[:, LP:T].rearrange("p (n t) -> p t n", t=CH)[:, 4 * k:4 * k + 4, :]
                            src = pt[k][:, :].rearrange("p (t n) -> p t n", t=4)
                        else:
                            out = go[:, 0:LP].rearrange("p (n t) -> p t n", t=CH)
                            src = pt[k][:, :].rearrange("p (t n) -> p t n", t=CH)
                        dve.tensor_copy(out, src).then_inc(go_done, 1)

            @block.tensor
            def _(pe):
                pe.sem_inc(y_mm, 8)
                pe.sem_inc(t_mm, 3)
                pe.wait_ge(const_in, 16)
                pe.wait_ge(t_in[0], 176)
                for _ in range(8):
                    pe.matmul(py[0][:, 0:2 * NC], ident[:, :], ut[0][:, 0, :], start=True, stop=True)
                with pe.Fori(0, NB // 2) as i:
                    for u in range(2):
                        pe.wait_ge(t_in[u], i * 176 + 176)
                        for k in range(4):
                            rows, first = (NCS, 0) if k < 2 else (NCP, NCS)
                            for g4 in range(4):
                                j, par = g4, k % 2
                                g = 2 * j + par
                                h = slice(64 * par, 64 * par + 64)
                                out = py[k][0:rows, g4 * TC:(g4 + 1) * TC]
                                pe.matmul(out, ut[u][:, j, par * NC + first:par * NC + first + rows], wt[u][:, g, :],
                                          start=True, stop=False, skip_group_check=True)
                                for x in range(4):
                                    dr, r = divmod(x, 2)
                                    at = GC * (1 - dr)
                                    mm = pe.matmul(out, hs[u][h, dr, r, j, first:first + rows], cp[u][h, dr, r, j, at:at + TC],
                                                   start=False, stop=(x == 3), skip_group_check=True)
                            mm.then_inc(y_mm, 1)
                        pe.wait_ge(g_done, i * 8 + 4 * (u + 1))
                        for t in range(CH):
                            mm = pe.transpose(pt[t // 4][:, (t % 4) * P:(t % 4 + 1) * P],
                                              ys[:, t, :, :].rearrange("p g c -> p (g c)"), ident[:, :])
                            if t % 4 == 3:
                                mm.then_inc(t_mm, 1)
                        for t in range(CH):
                            mm = pe.transpose(pt[2][:, t * NCP:(t + 1) * NCP],
                                              yp[:, t, :, :].rearrange("p g c -> p (g c)"), ident[0:NCP, 0:NCP])
                        mm.then_inc(t_mm, 1)


def glu(nc, d):
    NW, NG = D // W256, 6
    TG = NW * NG
    with Stage(nc, "gl") as s:
        ghi = s.sb("ghi", [P, KT, T], F32R)
        glo = s.sb("glo", [P, KT, T], F32R)
        raw = [s.sb(f"raw{u}", [P, T]) for u in range(2)]
        wraw = [s.sb(f"wraw{u}", [P, KT, W256]) for u in range(2)]
        whi = [s.sb(f"whi{u}", [P, KT, W256], F32R) for u in range(2)]
        wlo = [s.sb(f"wlo{u}", [P, KT, W256], F32R) for u in range(2)]
        gt = [s.sb(f"gt{k}", [P, 512]) for k in range(4)]
        za = [s.sb(f"za{k}", [P, 512]) for k in range(4)]
        sg = [s.sb(f"sg{k}", [P, 512]) for k in range(2)]
        ring = [s.ps(f"ring{k}", [P, 512]) for k in range(4)]

        raw_in = [s.sem(f"raw_in{u}") for u in range(2)]
        ghi_done, glo_done = s.sem("ghi_done"), s.sem("glo_done")
        w_in = [s.sem(f"w_in{u}") for u in range(2)]
        whi_done, w_ready = s.sem("whi_done"), s.sem("w_ready")
        grp_done, sg_done = s.sem("grp_done"), s.sem("sg_done")
        gz_in = [s.sem(f"gz_in{k}") for k in range(4)]
        gs_done, y_done = s.sem("gs_done"), s.sem("y_done")
        y_out = [s.sem(f"y_out{k}") for k in range(4)]
        w = d["e_w_glu"].rearrange("(k p) n -> p k n", p=P)

        def place(g):
            c = g % 3
            return slice((g // 3) * P, (g // 3 + 1) * P), slice(c * 512, (c + 1) * 512)

        with s.block() as block:

            @block.sync
            def _(sp):
                for k in range(KT):
                    if k >= 2:
                        sp.wait_ge(glo_done, k - 1)
                    sp.dma_start(raw[k % 2][:, :], d["gt"][k * P:(k + 1) * P, :]).then_inc(raw_in[k % 2], 16)
                    if k < 2:
                        sp.dma_start(wraw[k][:, :, :], w[:, :, k * W256:(k + 1) * W256]).then_inc(w_in[k], 16)
                for g in range(TG):
                    rows, cols = place(g)
                    if g >= 4:
                        sp.wait_ge(y_out[g % 4], 16 * (g // 4))
                    sp.dma_start(gt[g % 4][:, :], d["gt"][rows, cols]).then_inc(gz_in[g % 4], 16)
                    sp.dma_start(za[g % 4][:, :], d["za"][rows, cols]).then_inc(gz_in[g % 4], 16)
                    if g % NG == 0 and 2 <= g // NG + 1 < NW:
                        t = g // NG + 1
                        sp.wait_ge(w_ready, t - 1)
                        sp.dma_start(wraw[t % 2][:, :, :], w[:, :, t * W256:(t + 1) * W256]).then_inc(w_in[t % 2], 16)

            @block.gpsimd
            def _(pool):
                for t in range(NW):
                    u = t % 2
                    pool.wait_ge(w_in[u], 16 * (t // 2 + 1))
                    if t >= 2:
                        pool.wait_ge(grp_done, NG * (t - 1))
                    pool.tensor_copy(whi[u][:, :, :], wraw[u][:, :, :]).then_inc(whi_done, 1)
                    pool.wait_ge(whi_done, t + 1)
                    pool.tensor_tensor(wlo[u][:, :, :], wraw[u][:, :, :], whi[u][:, :, :].bitcast(F32),
                                       ALU.subtract).then_inc(w_ready, 1)

            @block.scalar
            def _(act):
                for k in range(KT):
                    act.wait_ge(raw_in[k % 2], 16 * (k // 2 + 1))
                    act.activation(ghi[:, k, :], raw[k % 2][:, :], ACT.Copy).then_inc(ghi_done, 1)
                for g in range(TG):
                    act.wait_ge(grp_done, g + 1)
                    if g >= 2:
                        act.wait_ge(gs_done, g - 1)
                    act.activation(sg[g % 2][:, :], ring[g % 4][:, :], ACT.Sigmoid).then_inc(sg_done, 1)
                    if g:
                        rows, cols = place(g - 1)
                        act.wait_ge(y_done, g)
                        act.dma_start(d["yt"][rows, cols], gt[(g - 1) % 4][:, :]).then_inc(y_out[(g - 1) % 4], 16)
                rows, cols = place(TG - 1)
                act.wait_ge(y_done, TG)
                act.dma_start(d["yt"][rows, cols], gt[(TG - 1) % 4][:, :]).then_inc(y_out[(TG - 1) % 4], 16)
                for k in range(4):
                    act.wait_ge(y_out[k], 16 * TG // 4)

            @block.vector
            def _(dve):
                for k in range(KT):
                    dve.wait_ge(ghi_done, k + 1)
                    dve.tensor_tensor(glo[:, k, :], raw[k % 2][:, :], ghi[:, k, :].bitcast(F32), ALU.subtract).then_inc(glo_done, 1)
                for g in range(TG):
                    dve.wait_ge(gz_in[g % 4], 32 * (g // 4 + 1))
                    dve.wait_ge(sg_done, g + 1)
                    dve.tensor_tensor(gt[g % 4][:, :], gt[g % 4][:, :], sg[g % 2][:, :], ALU.mult).then_inc(gs_done, 1)
                    dve.wait_ge(gs_done, g + 1)
                    dve.tensor_tensor(gt[g % 4][:, :], gt[g % 4][:, :], za[g % 4][:, :], ALU.mult).then_inc(y_done, 1)

            @block.tensor
            def _(pe):
                pe.wait_ge(glo_done, KT)
                for g in range(TG):
                    u = g // NG % 2
                    if g % NG == 0:
                        pe.wait_ge(w_ready, g // NG + 1)
                    if g >= 4:
                        pe.wait_ge(sg_done, g - 3)
                    h, c = divmod(g % NG, 3)
                    wc, tc = slice(h * P, (h + 1) * P), slice(c * 512, (c + 1) * 512)
                    for f in range(KT):
                        pe.matmul(ring[g % 4][:, :], whi[u][:, f, wc], ghi[:, f, tc], start=(f == 0), stop=False)
                        pe.matmul(ring[g % 4][:, :], whi[u][:, f, wc], glo[:, f, tc], start=False, stop=False)
                        mm = pe.matmul(ring[g % 4][:, :], wlo[u][:, f, wc], ghi[:, f, tc], start=False,
                                       stop=(f == KT - 1))
                    mm.then_inc(grp_done, 1)


def latent_projections(nc, d):
    PAIRS = HEADS // 2
    NN, NR, NK = 6, 3, 6
    PER = NN + NK + NT
    with Stage(nc, "lp") as s:
        chi = s.sb("chi", [P, 5, T], F32R)
        clo = s.sb("clo", [P, 5, T], F32R)
        krt = s.sb("krt", [P, T])
        ident = s.sb("ident", [P, P])
        gcol = s.sb("gcol", [P, 5])
        rope = s.sb("rope", [P, 2, T])
        ct = [s.sb(f"ct{u}", [P, CW]) for u in range(2)]
        rt = [s.sb(f"rt{u}", [P, 2 * ROPE]) for u in range(2)]
        kc = [s.sb(f"kc{u}", [P, 2, ROPE]) for u in range(2)]
        k2 = [s.sb(f"k2{u}", [P, 2, ROPE]) for u in range(2)]
        hf = [s.sb(f"hf{u}", [P, 5, P]) for u in range(2)]
        sq, sqk = s.sb("sq", [P, QL]), s.sb("sqk", [P, KVL])
        ss = [s.sb(f"ss{u}", [P, 8]) for u in range(2)]
        wraw = [s.sb(f"wraw{u}", [P, 5, 512]) for u in range(2)]
        whi = [s.sb(f"whi{u}", [P, 5, 512], F32R) for u in range(2)]
        wlo = [s.sb(f"wlo{u}", [P, 5, 512], F32R) for u in range(2)]
        stage = [s.sb(f"stage{k}", [P, 512]) for k in range(4)]
        r1, r2 = s.sb("r1", [P, 512]), s.sb("r2", [P, 512])
        r3 = [s.sb(f"r3{u}", [P, 512]) for u in range(2)]
        tp = [s.ps(f"tp{u}", [P, D]) for u in range(2)]
        ring = [s.ps(f"ring{k}", [P, 512]) for k in range(4)]

        const_in = s.sem("const_in")
        c_in = [s.sem(f"c_in{u}") for u in range(2)]
        c_free = s.sem("c_free")
        sq_done, ms_done, rt_done, rs_done, cn_done = (s.sem(x) for x in ("sq_done", "ms_done", "rt_done", "rs_done", "cn_done"))
        kc_done, k2_done, tp_done, hf_done, hi_done, lo_done = (
            s.sem(x) for x in ("kc_done", "k2_done", "tp_done", "hf_done", "hi_done", "lo_done"))
        w_in = [s.sem(f"w_in{u}") for u in range(2)]
        whi_done, w_ready, waited = s.sem("whi_done"), s.sem("w_ready"), s.sem("waited")
        grp_done, evac_done = s.sem("grp_done"), s.sem("evac_done")
        out_done = [s.sem(f"out_done{k}") for k in range(4)]
        rope_mm, rope_mul, rope_done = s.sem("rope_mm"), s.sem("rope_mul"), s.sem("rope_done")
        rope_out = [s.sem(f"rope_out{u}") for u in range(2)]
        kr_out = s.sem("kr_out")

        wn = d["w_uq_nope"].rearrange("(k p) n -> p k n", p=P)
        wr = d["w_uq_rope"].rearrange("(k p) n -> p k n", p=P)
        wsw = d["w_uq_swap"].rearrange("(k p) n -> p k n", p=P)
        wkv = d["e_w_ukv"].rearrange("(k p) n -> p k n", p=P)

        with s.block() as block:

            @block.sync
            def _(sp):
                sp.dma_start(ident[:, :], d["ident"][:, :]).then_inc(const_in, 16)
                sp.dma_start(gcol[:, 0:3], d["qn_col"][:, :]).then_inc(const_in, 16)
                sp.dma_start(gcol[:, 3:5], d["kvn_col"][:, :]).then_inc(const_in, 16)
                sp.dma_start(rope[:, :, :], d["rope_fm"].rearrange("a p t -> p a t")).then_inc(const_in, 16)
                with sp.Fori(0, NT // 2) as i:
                    for u in range(2):
                        rows = bass.ds(i * (2 * P) + u * P, P)
                        sp.wait_ge(c_free, i * 2 + (u + 1))
                        sp.dma_start(ct[u][:, :], d["cq"][rows, :]).then_inc(c_in[u], 16)
                        sp.dma_start(rt[u][:, :], d["rope_tm"][rows, :]).then_inc(c_in[u], 16)
                with sp.Fori(0, PAIRS // 2) as i:
                    for u in range(2):
                        sp.wait_ge(w_ready, i * 2 + (u + 1))
                        for dst, src in ((wraw[u][:, 0:3, 0:256], wn[:, :, bass.ds(i * 512 + u * 256, 256)]),
                                         (wraw[u][:, 0:3, 256:384], wr[:, :, bass.ds(i * 256 + u * 128, 128)]),
                                         (wraw[u][:, 0:3, 384:512], wsw[:, :, bass.ds(i * 256 + u * 128, 128)]),
                                         (wraw[u][:, 3:5, :], wkv[:, :, bass.ds(i * 1024 + u * 512, 512)])):
                            sp.dma_start(dst, src).then_inc(w_in[u], 16)
                    for u in range(2):
                        for c in range(NR):
                            b = (NR * u + c) % 2
                            sp.wait_ge(rope_done, i * (2 * NR) + NR * u + c + 2)
                            sp.dma_start(d["qr"][bass.ds(i * 256 + u * 128, P), c * 512:(c + 1) * 512], r3[b][:, :]).then_inc(rope_out[b], 16)
                sp.dma_start(d["kr"][:, :], krt[:, :]).then_inc(kr_out, 16)
                sp.wait_ge(kr_out, 16)
                for u in range(2):
                    sp.wait_ge(rope_out[u], 16 * (PAIRS * NR // 2 + 1))

            @block.gpsimd
            def _(pool):
                pool.sem_inc(w_ready, 2)
                pool.sem_inc(lo_done, 2)
                with pool.Fori(0, NT // 2) as i:
                    for u in range(2):
                        cols = bass.ds(i * (2 * P) + u * P, P)
                        pool.wait_ge(hi_done, i * 2 + (u + 1))
                        pool.tensor_tensor(clo[:, :, cols], hf[u][:, :, :], chi[:, :, cols].bitcast(F32),
                                           ALU.subtract).then_inc(lo_done, 1)
                with pool.Fori(0, PAIRS // 2) as i:
                    for u in range(2):
                        pool.wait_ge(w_in[u], i * 64 + 64)
                        pool.wait_ge(grp_done, i * (2 * PER) + PER * (u + 1))
                        pool.sem_inc(waited, 1)
                        pool.tensor_copy(whi[u][:, :, :], wraw[u][:, :, :]).then_inc(whi_done, 1)
                        pool.wait_ge(whi_done, i * 2 + (u + 1))
                        pool.tensor_tensor(wlo[u][:, :, :], wraw[u][:, :, :], whi[u][:, :, :].bitcast(F32),
                                           ALU.subtract).then_inc(w_ready, 1)

            @block.vector
            def _(dve):
                dve.sem_inc(c_free, 2)
                dve.sem_inc(rope_done, 1)
                dve.wait_ge(const_in, 64)
                H = ROPE // 2
                with dve.Fori(0, NT // 2) as i:
                    for u in range(2):
                        k = i * 2 + (u + 1)
                        st, kx = ss[u], ct[u][:, QL + KVL:CW]
                        dve.wait_ge(sq_done, i * 4 + 2 * (u + 1))
                        dve.tensor_scalar(st[:, 2:3], st[:, 0:1], 1.0 / QL, EPS, ALU.mult, ALU.add).then_inc(ms_done, 1)
                        dve.tensor_scalar(st[:, 3:4], st[:, 1:2], 1.0 / KVL, EPS, ALU.mult, ALU.add).then_inc(ms_done, 1)
                        dve.tensor_tensor(kc[u][:, 0, :], kx, rt[u][:, 0:ROPE], ALU.mult).then_inc(kc_done, 1)
                        dve.tensor_tensor(kc[u][:, 1, 0:H], kx[:, H:ROPE], rt[u][:, ROPE:ROPE + H], ALU.mult).then_inc(kc_done, 1)
                        dve.tensor_tensor(kc[u][:, 1, H:ROPE], kx[:, 0:H], rt[u][:, ROPE + H:2 * ROPE], ALU.mult).then_inc(kc_done, 1)
                        dve.wait_ge(rt_done, k)
                        dve.reciprocal(st[:, 6:8], st[:, 4:6]).then_inc(rs_done, 1)
                        dve.wait_ge(kc_done, i * 6 + 3 * (u + 1))
                        dve.tensor_tensor(k2[u][:, 0, :], kc[u][:, 0, :], kc[u][:, 1, :], ALU.add).then_inc(k2_done, 1)
                        dve.tensor_tensor(k2[u][:, 1, :], kc[u][:, 0, :], kc[u][:, 1, :], ALU.add).then_inc(k2_done, 1)
                        dve.wait_ge(rs_done, k)
                        dve.tensor_scalar(ct[u][:, 0:QL], ct[u][:, 0:QL], st[:, 6:7], None, ALU.mult).then_inc(cn_done, 1)
                        dve.tensor_scalar(ct[u][:, QL:QL + KVL], ct[u][:, QL:QL + KVL], st[:, 7:8], None, ALU.mult).then_inc(cn_done, 1)
                    for u in range(2):
                        k = i * 2 + (u + 1)
                        dve.wait_ge(tp_done, k)
                        dve.sem_inc(c_free, 1)
                        dve.wait_ge(lo_done, k)
                        dve.tensor_tensor(hf[u][:, 0:3, :], tp[u][:, 0:384].rearrange("p (k t) -> p k t", t=P),
                                          bc(gcol[:, 0:3], 2, P), ALU.mult).then_inc(hf_done, 1)
                        dve.tensor_tensor(hf[u][:, 3:5, :], tp[u][:, 512:768].rearrange("p (k t) -> p k t", t=P),
                                          bc(gcol[:, 3:5], 2, P), ALU.mult).then_inc(hf_done, 1)
                        dve.tensor_copy(krt[:, bass.ds(i * (2 * P) + u * P, P)], tp[u][:, 384:512]).then_inc(hf_done, 1)
                with dve.Fori(0, PAIRS // 2) as i:
                    for u in range(2):
                        for c in range(NR):
                            n, k = i * (2 * NR) + NR * u + c, NR * u + c
                            tc = slice(c * 512, (c + 1) * 512)
                            dve.wait_ge(rope_done, n + 1)
                            dve.wait_ge(rope_mm, n * 2 + 2)
                            dve.tensor_tensor(r1[:, :], tp[k % 2][:, 0:512], rope[:, 0, tc], ALU.mult).then_inc(rope_mul, 1)
                            dve.tensor_tensor(r2[:, :], tp[k % 2][:, 512:1024], rope[:, 1, tc], ALU.mult).then_inc(rope_mul, 1)
                            dve.wait_ge(rope_mul, n * 2 + 6)
                            dve.wait_ge(rope_out[k % 2], i * (16 * NR) + 16 * (k // 2 + 1))
                            dve.tensor_tensor(r3[k % 2][:, :], r1[:, :], r2[:, :], ALU.add).then_inc(rope_done, 1)

            @block.scalar
            def _(act):
                act.sem_inc(evac_done, 4)
                for u in range(2):
                    act.sem_inc(rope_out[u], 16)
                for k in range(4):
                    act.sem_inc(out_done[k], 16)
                with act.Fori(0, NT // 2) as i:
                    for u in range(2):
                        k = i * 2 + (u + 1)
                        act.wait_ge(c_in[u], i * 32 + 32)
                        act.activation(sq[:, :], ct[u][:, 0:QL], ACT.Square, accum_out=ss[u][:, 0:1]).then_inc(sq_done, 1)
                        act.activation(sqk[:, :], ct[u][:, QL:QL + KVL], ACT.Square, accum_out=ss[u][:, 1:2]).then_inc(sq_done, 1)
                        act.wait_ge(ms_done, i * 4 + 2 * (u + 1))
                        act.activation(ss[u][:, 4:6], ss[u][:, 2:4], ACT.Sqrt).then_inc(rt_done, 1)
                    for u in range(2):
                        act.wait_ge(hf_done, i * 6 + 3 * (u + 1))
                        act.activation(chi[:, :, bass.ds(i * (2 * P) + u * P, P)], hf[u][:, :, :], ACT.Copy).then_inc(hi_done, 1)
                with act.Fori(0, PAIRS // 2) as i:
                    for u in range(2):
                        def store(k):
                            g = PER * u + k
                            act.wait_ge(evac_done, i * (2 * PER) + g + 5)
                            if k < NN + NK:
                                h, c = divmod(k % NN, 3)
                                out = (d["qn"] if k < NN else d["kn"])[bass.ds(i * 512 + (2 * u + h) * P, P), c * 512:(c + 1) * 512]
                                src = stage[g % 4][:, :]
                            else:
                                t = k - NN - NK
                                out = d["v"][t * P:(t + 1) * P, bass.ds(i * 512 + u * 256, 256)]
                                src = stage[g % 4][:, 0:256]
                            act.dma_start(out, src).then_inc(out_done[g % 4], 16)

                        for k in range(PER):
                            g = PER * u + k
                            cols = 512 if k < NN + NK else 256
                            act.wait_ge(grp_done, i * (2 * PER) + (g + 1 + 2 * PER))
                            act.wait_ge(out_done[g % 4], i * (8 * PER) + 16 * (g // 4 + 1))
                            act.activation(stage[g % 4][:, 0:cols], ring[g % 4][:, 0:cols], ACT.Copy).then_inc(evac_done, 1)
                            if k:
                                store(k - 1)
                        store(PER - 1)
                for k in range(4):
                    act.wait_ge(out_done[k], 16 * (PAIRS * PER // 4 + 1))

            @block.tensor
            def _(pe):
                pe.sem_inc(grp_done, 2 * PER)
                pe.sem_inc(rope_mul, 4)
                pe.wait_ge(const_in, 64)
                with pe.Fori(0, NT // 2) as i:
                    for u in range(2):
                        pe.wait_ge(cn_done, i * 4 + 2 * (u + 1))
                        pe.wait_ge(k2_done, i * 4 + 2 * (u + 1))
                        for k, at in enumerate((0, 128, 256, 512, 640)):
                            pe.transpose(tp[u][:, at:at + P], ct[u][:, k * P:(k + 1) * P], ident[:, :])
                        pe.transpose(tp[u][:, 384:512], k2[u][:, :, :].rearrange("p a b -> p (a b)"), ident[:, :]).then_inc(tp_done, 1)
                pe.wait_ge(lo_done, NT + 2)
                pe.wait_ge(hf_done, 3 * NT)

                def sums(out, tiles, lhs, rhs):
                    for n, k in enumerate(tiles):
                        (ah, al), (bh, bl) = lhs(k), rhs(k)
                        pe.matmul(out, ah, bh, start=(n == 0), stop=False)
                        pe.matmul(out, ah, bl, start=False, stop=False)
                        mm = pe.matmul(out, al, bh, start=False, stop=(n == len(tiles) - 1))
                    return mm

                with pe.Fori(0, PAIRS // 2) as i:
                    for u in range(2):
                        pe.wait_ge(w_ready, i * 2 + (u + 3))

                        def w(cols):
                            return lambda k: (whi[u][:, k, cols], wlo[u][:, k, cols])

                        def c(cols):
                            return lambda k: (chi[:, k, cols], clo[:, k, cols])

                        for r in range(NR):
                            k = NR * u + r
                            pe.wait_ge(rope_mul, i * (4 * NR) + 2 * k + 2)
                            tc = slice(r * 512, (r + 1) * 512)
                            for half in range(2):
                                sums(tp[k % 2][:, half * 512:(half + 1) * 512], range(3),
                                     w(slice(256 + 128 * half, 384 + 128 * half)), c(tc)).then_inc(rope_mm, 1)
                        for k in range(PER):
                            g = PER * u + k
                            pe.wait_ge(evac_done, i * (2 * PER) + g + 1)
                            if k < NN + NK:
                                h, cc = divmod(k % NN, 3)
                                tc = slice(cc * 512, (cc + 1) * 512)
                                if k < NN:
                                    mm = sums(ring[g % 4][:, :], range(3), w(slice(h * P, (h + 1) * P)), c(tc))
                                else:
                                    mm = sums(ring[g % 4][:, :], range(3, 5), w(slice(h * 256, h * 256 + P)), c(tc))
                            else:
                                t = k - NN - NK

                                def vw(x):
                                    return x.rearrange("p (h a) -> p h a", h=2)[:, :, P:2 * P]
                                mm = sums(ring[g % 4][:, 0:256].rearrange("p (h a) -> p h a", h=2), range(3, 5),
                                          c(slice(t * P, (t + 1) * P)), lambda k: (vw(whi[u][:, k, :]), vw(wlo[u][:, k, :])))
                            mm.then_inc(grp_done, 1)


def attention(nc, d):
    tiles = [(h, t0 // P + n, t0, ln) for h in range(2) for t0, ln in SEQS for n in range(ln // P)]
    NQ = len(tiles)
    NP = NQ // 2
    STEPS = HEADS // 2
    first = [0]
    for x in tiles:
        first.append(first[-1] + x[3] // 512)
    NG = first[-1]

    def group(n):
        return n // NQ * NG + first[n % NQ]

    def groups(n):
        return tiles[n % NQ][3] // 512

    def pipelined(eng, front, middle, back):
        for n in range(4):
            if n >= 2:
                middle(0, n - 2)
            front(0, n)
        with eng.Fori(0, STEPS - 1) as i:
            for n in range(4, NQ + 4):
                middle(i, n - 2)
                front(i, n)
                if n % 2 == 0:
                    back(i, n // 2 - 2)
        for n in range(4, NQ + 4):
            if n - 2 < NQ:
                middle(STEPS - 1, n - 2)
            if n < NQ:
                front(STEPS - 1, n)
            if n % 2 == 0:
                back(STEPS - 1, n // 2 - 2)

    with Stage(nc, "at") as s:
        ident = s.sb("ident", [P, P])
        krh = s.sb("krh", [P, T], F32R)
        krl = s.sb("krl", [P, T], F32R)
        qr = [s.sb(f"qr{h}", [P, T], F32R) for h in range(2)]
        qnh, qnl, knh, knl = ([s.sb(f"{x}{h}", [P, T], F32R) for h in range(2)] for x in ("qnh", "qnl", "knh", "knl"))
        vh, vl = ([s.sb(f"{x}{h}", [P, NT, VD], F32R) for h in range(2)] for x in ("vh", "vl"))
        raw = [s.sb(f"raw{x}", [P, T]) for x in range(4)]
        zb = [s.sb(f"zb{h}", [P, T]) for h in range(2)]
        y = [s.sb(f"y{h}", [P, T]) for h in range(2)]
        pr = [s.sb(f"pr{u}", [P, LS]) for u in range(3)]
        pth, ptl = ([s.sb(f"{x}{u}", [P, LS // P, 2, P], F32R) for u in range(2)] for x in ("pth", "ptl"))
        st = [s.sb(f"st{u}", [P, 4]) for u in range(3)]
        sc = [s.ps(f"sc{u}", [P, LS]) for u in range(2)]
        tr = [s.ps(f"tr{u}", [P, 512]) for u in range(2)]
        o = [s.ps(f"o{u}", [P, 512]) for u in range(2)]

        const_in, kr_hi, kr_split = (s.sem(x) for x in ("const_in", "kr_hi", "kr_split"))
        raw_in = [s.sem(f"raw_in{x}") for x in range(4)]
        z_in = [s.sem(f"z_in{h}") for h in range(2)]
        rnd_done, split_done, first_hi = s.sem("rnd_done"), s.sem("split_done"), s.sem("first_hi")
        sc_done, mx_done, nm_done, exp_done, rs_done, pr_done, tr_done, hi_done, lo_done, o_done, y_done, waited = (
            s.sem(x) for x in ("sc_done", "mx_done", "nm_done", "exp_done", "rs_done", "pr_done", "tr_done", "hi_done",
                               "lo_done", "o_done", "y_done", "waited"))
        y_out = [s.sem(f"y_out{h}") for h in range(2)]

        with s.block() as block:

            @block.sync
            def _(sp):
                sp.dma_start(ident[:, :], d["ident"][:, :]).then_inc(const_in, 16)
                sp.dma_start(raw[3][:, :], d["kr"][:, :]).then_inc(const_in, 16)
                with sp.Fori(0, STEPS) as i:
                    for h in range(2):
                        rows = bass.ds(i * 256 + h * P, P)
                        rope = bass.ds(i * P + h * ROPE, ROPE)
                        for x, parts in enumerate((((raw[0][:, :], d["kn"][rows, :]),), ((raw[1][:, :], d["qn"][rows, :]),),
                                                   ((raw[2][0:64, :], d["qr"][rope, :]), (raw[2][64:P, :], d["qr"][rope, :])),
                                                   ((raw[3][:, :].rearrange("p (n v) -> p n v", v=VD),
                                                     d["v"][:, rows].rearrange("(n p) v -> p n v", p=P)),))):
                            sp.wait_ge(split_done, i * 8 + (4 * h + x + 1))
                            if x == 3:
                                sp.wait_ge(kr_split, 1)
                            sp.sem_inc(waited, 1)
                            for dst, src in parts:
                                sp.dma_start(dst, src).then_inc(raw_in[x], 16)
                        sp.wait_ge(y_done, i * NP + (NP // 2) * (h + 1))
                        sp.sem_inc(waited, 1)
                        sp.dma_start(zb[h][:, :], d["zb"][rows, :]).then_inc(z_in[h], 16)

            @block.gpsimd
            def _(pool):
                pool.sem_inc(split_done, 4)
                for h in range(2):
                    pool.sem_inc(y_out[h], 16)
                pool.wait_ge(const_in, 32)
                pool.sem_inc(rnd_done, 2)
                pool.tensor_copy(krh[:, :], raw[3][:, :]).then_inc(kr_hi, 1)
                pool.wait_ge(kr_hi, 1)
                pool.tensor_tensor(krl[:, :], raw[3][:, :], krh[:, :].bitcast(F32), ALU.subtract).then_inc(kr_split, 1)

                def split(i, h, x, first=False):
                    hi, lo = ((knh, knl), (qnh, qnl), (qr, qr), (vh, vl))[x]
                    if x == 0:
                        pool.wait_ge(sc_done, i * NQ + (NQ // 2) * (h + 1))
                    if x == 3:
                        pool.wait_ge(o_done, i * NP + (NP // 2) * (h + 1))
                        pool.wait_ge(split_done, i * 8 + (4 * h + 7))
                    per = 32 if x == 2 else 16
                    pool.wait_ge(raw_in[x], i * (2 * per) + per * (h + 1))
                    pool.sem_inc(waited, 1)
                    rows = slice(64, P) if x == 2 else slice(0, P)
                    if x == 3:
                        a, b, c = hi[h][:, :, :], lo[h][:, :, :], raw[x][:, :].rearrange("p (n v) -> p n v", v=VD)
                        pool.tensor_copy(a, c).then_inc(rnd_done, 1)
                    else:
                        a, b, c = hi[h][rows, :], lo[h][rows, :], raw[x][rows, :]
                        pool.tensor_copy(hi[h][:, :], raw[x][:, :]).then_inc(rnd_done, 1)
                    pool.wait_ge(rnd_done, i * 8 + (4 * h + x + 1))
                    if first:
                        pool.wait_ge(split_done, 6)
                    pool.tensor_tensor(b, c, a.bitcast(F32), ALU.subtract).then_inc(split_done, 1)

                for x in (2, 3):
                    split(0, 0, x, x == 2)
                with pool.Fori(0, STEPS - 1) as i:
                    for h in (1, 2):
                        for x in range(4):
                            split(i if h == 1 else i + 1, h % 2, x)
                for x in range(4):
                    split(STEPS - 1, 1, x)

            @block.scalar
            def _(act):
                def front(i, n):
                    u, ln = n % 3, tiles[n % NQ][3]
                    act.wait_ge(nm_done, i * NQ + (n + 1))
                    if n >= 3:
                        act.wait_ge(tr_done, i * NG + group(n - 2))
                    act.activation(pr[u][:, 0:ln], sc[n % 2][:, 0:ln], ACT.Exp, bias=st[u][:, 1:2],
                                   scale=MLA_SCALE, accum_out=st[u][:, 2:3]).then_inc(exp_done, 1)
                    act.wait_ge(rs_done, i * NQ + (n + 1))
                    act.activation(pr[u][:, 0:ln], pr[u][:, 0:ln], ACT.Copy, scale=st[u][:, 3:4]).then_inc(pr_done, 1)

                def middle(i, n):
                    m = n // 2
                    for g in range(groups(n)):
                        act.wait_ge(tr_done, i * NG + (group(n) + g + 1))
                        if m >= 2:
                            act.wait_ge(o_done, i * NP + (m - 1 + NP))
                        act.activation(pth[m % 2][:, 4 * g:4 * g + 4, n % 2, :],
                                       tr[(group(n) + g) % 2][:, :].rearrange("p (c q) -> p c q", q=P), ACT.Copy).then_inc(hi_done, 1)
                    if n in (NQ // 2 + 3, NQ + 1):
                        h = int(n > NQ)
                        act.wait_ge(y_done, i * NP + ((h + 1) * NP // 2 + NP))
                        act.dma_start(d["yt"][bass.ds(i * 256 + (D + h * P), P), :], y[h][:, :]).then_inc(y_out[h], 16)

                def back(i, m):
                    pass

                for x, hi in enumerate((knh, qnh)):
                    act.wait_ge(raw_in[x], 16)
                    act.activation(hi[0][:, :], raw[x][:, :], ACT.Copy).then_inc(first_hi, 1)
                pipelined(act, front, middle, back)
                act.wait_ge(y_done, STEPS * NP + NP)
                act.dma_start(d["yt"][2 * D - P:2 * D, :], y[1][:, :]).then_inc(y_out[1], 16)
                for h in range(2):
                    act.wait_ge(y_out[h], 16 * (STEPS + 1))

            @block.vector
            def _(dve):
                dve.sem_inc(y_done, NP)
                for x, (hi, lo) in enumerate(((knh, knl), (qnh, qnl))):
                    dve.wait_ge(first_hi, x + 1)
                    dve.tensor_tensor(lo[0][:, :], raw[x][:, :], hi[0][:, :].bitcast(F32), ALU.subtract).then_inc(split_done, 1)

                def front(i, n):
                    b, ln = st[n % 3], tiles[n % NQ][3]
                    dve.wait_ge(sc_done, i * NQ + (n + 1 + NQ))
                    dve.tensor_reduce(b[:, 0:1], sc[n % 2][:, 0:ln], AX_X, ALU.max).then_inc(mx_done, 1)
                    dve.wait_ge(mx_done, i * NQ + (n + 1))
                    dve.tensor_scalar(b[:, 1:2], b[:, 0:1], -MLA_SCALE, None, ALU.mult).then_inc(nm_done, 1)
                    if n >= 2:
                        lows(i, n - 2)
                    dve.wait_ge(exp_done, i * NQ + (n + 1))
                    dve.reciprocal(b[:, 3:4], b[:, 2:3]).then_inc(rs_done, 1)

                def lows(i, n):
                    m = n // 2
                    for g in range(groups(n)):
                        dve.wait_ge(hi_done, i * NG + (group(n) + g + 1))
                        dve.tensor_tensor(ptl[m % 2][:, 4 * g:4 * g + 4, n % 2, :],
                                          tr[(group(n) + g) % 2][:, :].rearrange("p (c q) -> p c q", q=P),
                                          pth[m % 2][:, 4 * g:4 * g + 4, n % 2, :].bitcast(F32), ALU.subtract).then_inc(lo_done, 1)

                def middle(i, n):
                    if isinstance(i, int) and i == STEPS - 1 and n >= NQ - 2:
                        lows(i, n)

                def back(i, m):
                    h, t, _, _ = tiles[2 * m]
                    dve.wait_ge(o_done, i * NP + (m + 1 + NP))
                    if m % (NP // 2) == 0:
                        dve.wait_ge(z_in[h], i * 16 + 16)
                        dve.wait_ge(y_out[h], i * 16 + 16)
                    dve.tensor_tensor(y[h][:, t * P:(t + 2) * P], o[m % 2][:, 0:2 * P], zb[h][:, t * P:(t + 2) * P],
                                      ALU.mult).then_inc(y_done, 1)

                pipelined(dve, front, middle, back)

            @block.tensor
            def _(pe):
                pe.sem_inc(sc_done, NQ)
                pe.sem_inc(o_done, NP)
                pe.wait_ge(const_in, 32)
                pe.wait_ge(kr_split, 1)

                def front(i, n):
                    h, t, t0, ln = tiles[n % NQ]
                    q = slice(t * P, (t + 1) * P)
                    if n % (NQ // 2) == 0:
                        pe.wait_ge(split_done, i * 8 + (4 * (n // (NQ // 2)) + 3 + 4))
                    if n >= 2:
                        pe.wait_ge(exp_done, i * NQ + (n - 1))
                    for c in range(ln // 512):
                        out, k = sc[n % 2][:, c * 512:(c + 1) * 512], slice(t0 + c * 512, t0 + (c + 1) * 512)
                        pe.matmul(out, qnh[h][:, q], knh[h][:, k], start=True, stop=False)
                        pe.matmul(out, qnh[h][:, q], knl[h][:, k], start=False, stop=False)
                        pe.matmul(out, qnl[h][:, q], knh[h][:, k], start=False, stop=False)
                        pe.matmul(out, qr[h][:, q], krh[:, k], start=False, stop=False)
                        mm = pe.matmul(out, qr[h][0:64, q], krl[0:64, k], start=False, stop=True)
                    mm.then_inc(sc_done, 1)

                def middle(i, n):
                    pe.wait_ge(pr_done, i * NQ + (n + 1))
                    for g in range(groups(n)):
                        if group(n) + g >= 2:
                            pe.wait_ge(lo_done, i * NG + (group(n) + g - 1))
                        for c in range(4):
                            mm = pe.transpose(tr[(group(n) + g) % 2][:, c * P:(c + 1) * P],
                                              pr[n % 3][:, (4 * g + c) * P:(4 * g + c + 1) * P], ident[:, :])
                        mm.then_inc(tr_done, 1)

                def back(i, m):
                    h, t, t0, ln = tiles[2 * m]
                    pe.wait_ge(lo_done, i * NG + group(2 * m + 2))
                    if m % (NP // 2) == 0:
                        pe.wait_ge(split_done, i * 8 + (4 * h + 4 + 4))
                    pe.wait_ge(y_done, i * NP + (m - 1 + NP))
                    nb = ln // P
                    for c in range(nb):
                        for k, (a, b) in enumerate(((vh, pth), (vh, ptl), (vl, pth))):
                            mm = pe.matmul(o[m % 2][:, 0:2 * P], a[h][:, t0 // P + c, :],
                                           b[m % 2][:, c, :, :].rearrange("p a q -> p (a q)"),
                                           start=(c == 0 and k == 0), stop=(c == nb - 1 and k == 2))
                    mm.then_inc(o_done, 1)

                pipelined(pe, front, middle, back)


def out_projection(nc, d, tag, w_out, post, segments):
    KO = 2 * D // P
    with Stage(nc, tag) as s:
        whi = s.sb("whi", [P, KO, D], F32R)
        wlo = s.sb("wlo", [P, KO, D], F32R)
        raw = [s.sb(f"raw{u}", [P, KO, P]) for u in range(2)]
        yhi = [s.sb(f"yhi{u}", [P, KO, P], F32R) for u in range(2)]
        ylo = [s.sb(f"ylo{u}", [P, KO, P], F32R) for u in range(2)]
        xt = [s.sb(f"xt{u}", [P, D]) for u in range(2)]
        tmp = s.sb("tmp", [P, D])
        gain = s.sb("gain", [P, D])
        ss = [s.sb(f"ss{u}", [P, 4]) for u in range(2)]
        acc = [s.ps(f"acc{u}", [P, D]) for u in range(2)]
        const_in = s.sem("const_in")
        w_in = [s.sem(f"w_in{u}") for u in range(2)]
        whi_done, wlo_done = s.sem("whi_done"), s.sem("wlo_done")
        y_in = [s.sem(f"y_in{u}") for u in range(2)]
        x_in = [s.sem(f"x_in{u}") for u in range(2)]
        yhi_done, ylo_done, mm_done, sq_done, ms_done, rt_done, rs_done, n_done, out_ready = (
            s.sem(x) for x in ("yhi_done", "ylo_done", "mm_done", "sq_done", "ms_done", "rt_done", "rs_done", "n_done", "out_ready"))
        out_done = [s.sem(f"out_done{u}") for u in range(2)]
        waited = s.sem("waited")
        w = w_out.rearrange("(k p) n -> p k n", p=P)
        NWC = KO // 2
        segs, first = [], 0
        for x, out, t0, n in segments:
            segs.append((x, out, t0, n, first))
            first += n
        total = first
        yt = d["yt"].rearrange("(k p) t -> p k t", p=P)

        with s.block() as block:

            @block.sync
            def _(sp):
                sp.dma_start(gain[:, :], post.partition_broadcast(P)).then_inc(const_in, 16)
                t0 = segs[0][2]
                for u in range(2):
                    sp.dma_start(raw[u][:, :, :], yt[:, :, (t0 + u) * P:(t0 + u + 1) * P]).then_inc(y_in[u], 16)
                for c in range(NWC):
                    if c >= 2:
                        sp.wait_ge(wlo_done, c - 1)
                    else:
                        sp.wait_ge(ylo_done, c + 3)
                    sp.dma_start(raw[c % 2][:, :, :].rearrange("p k n -> p (k n)").rearrange("p (k n) -> p k n", k=2),
                                 w[:, 2 * c:2 * c + 2, :]).then_inc(w_in[c % 2], 16)
                for u in range(2):
                    sp.wait_ge(out_done[u], 16)
                    sp.dma_start(xt[u][:, :], segs[0][0][u * P:(u + 1) * P, :]).then_inc(x_in[u], 16)
                sp.wait_ge(wlo_done, NWC)
                for x, out, t0, n, f in segs:
                    with sp.Fori(int(f == 0), n // 2) as i:
                        for u in range(2):
                            sp.wait_ge(ylo_done, i * 2 + (f + u + 1))
                            sp.dma_start(raw[u][:, :, :], yt[:, :, bass.ds(i * (2 * P) + (t0 + u) * P, P)]).then_inc(y_in[u], 16)
                            sp.wait_ge(out_done[u], i * 16 + 16 * (f // 2 + 1))
                            sp.dma_start(xt[u][:, :], x[bass.ds(i * (2 * P) + u * P, P), :]).then_inc(x_in[u], 16)

            @block.gpsimd
            def _(pool):
                pool.sem_inc(ylo_done, 2)
                pool.sem_inc(mm_done, 2)
                for x, out, t0, n, f in segs:
                    with pool.Fori(int(f == 0), n // 2) as i:
                        for u in range(2):
                            k = i * 2 + (f + u + 1)
                            pool.wait_ge(y_in[u], i * 16 + 16 * (f // 2 + 1))
                            pool.wait_ge(mm_done, k)
                            pool.sem_inc(waited, 1)
                            pool.tensor_copy(yhi[u][:, :, :], raw[u][:, :, :]).then_inc(yhi_done, 1)
                            pool.wait_ge(yhi_done, k)
                            pool.tensor_tensor(ylo[u][:, :, :], raw[u][:, :, :], yhi[u][:, :, :].bitcast(F32),
                                               ALU.subtract).then_inc(ylo_done, 1)

            @block.scalar
            def _(act):
                for u in range(2):
                    act.wait_ge(y_in[u], 16)
                    act.activation(yhi[u][:, :, :], raw[u][:, :, :], ACT.Copy).then_inc(yhi_done, 1)
                for c in range(NWC):
                    act.wait_ge(w_in[c % 2], 16 * (c // 2 + 1))
                    act.activation(whi[:, 2 * c:2 * c + 2, :].rearrange("p k n -> p (k n)"),
                                   raw[c % 2][:, :, :].rearrange("p k n -> p (k n)"), ACT.Copy).then_inc(whi_done, 1)
                for x, out, t0, n, f in segs:
                    with act.Fori(0, n // 2) as i:
                        for u in range(2):
                            k = i * 2 + (f + u + 1)
                            act.wait_ge(mm_done, k + 2)
                            act.wait_ge(out_ready, k)
                            act.activation(tmp[:, :], acc[u][:, :], ACT.Square, accum_out=ss[u][:, 0:1]).then_inc(sq_done, 1)
                            act.wait_ge(ms_done, k)
                            act.activation(ss[u][:, 2:3], ss[u][:, 1:2], ACT.Sqrt).then_inc(rt_done, 1)
                            act.wait_ge(out_ready, k + 1)
                            act.dma_start(out[bass.ds(i * (2 * P) + u * P, P), :], xt[u][:, :]).then_inc(out_done[u], 16)
                for u in range(2):
                    act.wait_ge(out_done[u], 16 * (total // 2 + 1))

            @block.vector
            def _(dve):
                dve.sem_inc(n_done, 2)
                dve.sem_inc(out_ready, 1)
                for u in range(2):
                    dve.sem_inc(out_done[u], 16)
                for u in range(2):
                    dve.wait_ge(yhi_done, u + 1)
                    dve.tensor_tensor(ylo[u][:, :, :], raw[u][:, :, :], yhi[u][:, :, :].bitcast(F32), ALU.subtract).then_inc(ylo_done, 1)
                for c in range(NWC):
                    dve.wait_ge(whi_done, c + 1)
                    dve.tensor_tensor(wlo[:, 2 * c:2 * c + 2, :].rearrange("p k n -> p (k n)"),
                                      raw[c % 2][:, :, :].rearrange("p k n -> p (k n)"),
                                      whi[:, 2 * c:2 * c + 2, :].rearrange("p k n -> p (k n)").bitcast(F32),
                                      ALU.subtract).then_inc(wlo_done, 1)
                dve.wait_ge(const_in, 16)
                for x, out, t0, n, f in segs:
                    with dve.Fori(0, n // 2) as i:
                        for u in range(2):
                            k = i * 2 + (f + u + 1)
                            st = ss[u]
                            dve.wait_ge(sq_done, k)
                            dve.tensor_scalar(st[:, 1:2], st[:, 0:1], 1.0 / D, EPS, ALU.mult, ALU.add).then_inc(ms_done, 1)
                            dve.wait_ge(rt_done, k)
                            dve.reciprocal(st[:, 3:4], st[:, 2:3]).then_inc(rs_done, 1)
                            dve.wait_ge(rs_done, k)
                            dve.scalar_tensor_tensor(tmp[:, :], acc[u][:, :], st[:, 3:4], gain[:, :], ALU.mult,
                                                     ALU.mult).then_inc(n_done, 1)
                            dve.wait_ge(n_done, k + 2)
                            dve.wait_ge(x_in[u], i * 16 + 16 * (f // 2 + 1))
                            dve.tensor_tensor(xt[u][:, :], xt[u][:, :], tmp[:, :], ALU.add).then_inc(out_ready, 1)

            @block.tensor
            def _(pe):
                def sums(u, tiles):
                    for h in range(2):
                        c = slice(h * 512, (h + 1) * 512)
                        for f2 in tiles:
                            pe.matmul(acc[u][:, c], yhi[u][:, f2, :], whi[:, f2, c], start=(f2 == 0), stop=False)
                            pe.matmul(acc[u][:, c], yhi[u][:, f2, :], wlo[:, f2, c], start=False, stop=False)
                            mm = pe.matmul(acc[u][:, c], ylo[u][:, f2, :], whi[:, f2, c], start=False, stop=(f2 == KO - 1))
                    return mm

                pe.wait_ge(ylo_done, 4)
                pe.wait_ge(n_done, 2)
                for c in range(NWC):
                    pe.wait_ge(wlo_done, c + 1)
                    for u in range(2):
                        mm = sums(u, (2 * c, 2 * c + 1))
                        if c == NWC - 1:
                            mm.then_inc(mm_done, 1)
                for x, out, t0, n, f in segs:
                    with pe.Fori(int(f == 0), n // 2) as i:
                        for u in range(2):
                            k = i * 2 + (f + u + 1)
                            pe.wait_ge(ylo_done, k + 2)
                            pe.wait_ge(n_done, k)
                            sums(u, range(KO)).then_inc(mm_done, 1)


def even_out_projection(nc, d):
    out_projection(nc, d, "eo", d["e_w_out"], d["post_norm"][0],
                   ((d["x_prompt"], d["x1"][0:LP, :], 0, LP // P), (d["x_sample"], d["x1"][LP:T, :], LP // P, LS // P)))


def even_layer(nc, d):
    even_input_projection(nc, d)
    s5(nc, d)
    glu(nc, d)
    latent_projections(nc, d)
    attention(nc, d)
    even_out_projection(nc, d)


def odd_input_projection(nc, d):
    w = d["o_w_in"].rearrange("(k p) n -> p k n", p=P)
    gw = d["gate_w"].rearrange("(k p) n -> p k n", p=P)

    def fm(col, dst):
        return ("fm", lambda i: w[:, :, bass.ds(i * W256 + col, W256)], W256, ACT.Copy,
                lambda i, h: dst[bass.ds(i * W256 + h * P, P), :])

    def tm(col, func, at):
        return ("tm", lambda i: w[:, :, bass.ds(i * W256 + col, W256)], W256, func,
                lambda i, h: d["tmo"][:, bass.ds(i * W256 + at, W256)])

    norm_and_project(
        nc, d, "oi", ((d["x1"], NT),), d["pre_col"][1],
        (
            (D // W256, (fm(O_U, d["uc"]), fm(O_Q, d["qkd"]))),
            (D // W256, (tm(O_V, ACT.Copy, 0), tm(O_O, ACT.Sigmoid, D), tm(O_Z, ACT.Silu, 2 * D), tm(O_VD, ACT.Copy, 3 * D))),
            (1, tuple(tm(O_ZD + c * W256, ACT.Silu, 4 * D + c * W256) for c in range(D // W256)) + (
                ("fm1", lambda i: gw, P, ACT.Copy, lambda i, h: d["gg"]),)),
        ))


def conv_and_qk(nc, d):
    with Stage(nc, "cv") as s:
        u_ = [s.sb(f"u{b}", [P, 2, T]) for b in range(2)]
        acc = [s.sb(f"acc{b}", [P, 2, T]) for b in range(2)]
        ahi = [s.sb(f"ahi{b}", [P, 2, T], F32R) for b in range(2)]
        alo = [s.sb(f"alo{b}", [P, 2, T], F32R) for b in range(2)]
        wraw = [s.sb(f"wraw{b}", [P, 2, 512]) for b in range(2)]
        whi = [s.sb(f"whi{b}", [P, 2, 512], F32R) for b in range(2)]
        wlo = [s.sb(f"wlo{b}", [P, 2, 512], F32R) for b in range(2)]
        cw = [s.sb(f"cw{b}", [P, 2, 4]) for b in range(2)]
        stage = [s.sb(f"stage{k}", [P, 512]) for k in range(4)]
        ring = [s.ps(f"ring{k}", [P, 512]) for k in range(4)]
        u_in = [s.sem(f"u_in{b}") for b in range(2)]
        tap1, tap2, tap3, a_done, ahi_done, alo_done, whi_done, wlo_done, grp_done, evac_done = (
            s.sem(x) for x in ("tap1", "tap2", "tap3", "a_done", "ahi_done", "alo_done", "whi_done", "wlo_done", "grp_done", "evac_done"))
        out_done = [s.sem(f"out_done{k}") for k in range(4)]
        NG = 12

        with s.block() as block:

            @block.sync
            def _(sp):
                for h in range(MH):
                    b = h % 2
                    if h >= 2:
                        sp.wait_ge(alo_done, h - 1)
                        sp.wait_ge(wlo_done, h - 1)
                    sp.dma_start(u_[b][:, :, :], d["uc"][h * MD:(h + 1) * MD, :].rearrange("(k p) t -> p k t", p=P)).then_inc(u_in[b], 16)
                    sp.dma_start(cw[b][:, :, :], d["conv_col"][:, 2 * h:2 * h + 2, :]).then_inc(u_in[b], 16)
                    sp.dma_start(wraw[b][:, :, 0:256], d["o_w_q"][h].rearrange("(k p) e -> p k e", p=P)).then_inc(u_in[b], 16)
                    sp.dma_start(wraw[b][:, :, 256:512], d["o_w_k"][h].rearrange("(k p) e -> p k e", p=P)).then_inc(u_in[b], 16)

            @block.vector
            def _(dve):
                n = 0
                for h in range(MH):
                    b = h % 2
                    dve.wait_ge(u_in[b], 64 * (h // 2 + 1))
                    if h >= 2:
                        dve.wait_ge(alo_done, h - 1)
                    for k in range(2):
                        x, y, w = u_[b][:, k, :], acc[b][:, k, :], cw[b][:, k, :]
                        dve.tensor_scalar(y, x, w[:, 1:2], None, ALU.mult).then_inc(tap1, 1)
                    for k in range(2):
                        x, y, w = u_[b][:, k, :], acc[b][:, k, :], cw[b][:, k, :]
                        dve.wait_ge(tap1, 2 * h + k + 1)
                        for t0, ln in SEQS:
                            a, e = t0, t0 + ln
                            dve.scalar_tensor_tensor(y[:, a + 1:e], x[:, a:e - 1], w[:, 0:1], y[:, a + 1:e], ALU.mult, ALU.add).then_inc(tap2, 1)
                    for k in range(2):
                        x, y, w = u_[b][:, k, :], acc[b][:, k, :], cw[b][:, k, :]
                        dve.wait_ge(tap2, 4 * h + 2 * k + 2)
                        for t0, ln in SEQS:
                            a, e = t0, t0 + ln
                            dve.scalar_tensor_tensor(y[:, a:e - 1], x[:, a + 1:e], w[:, 2:3], y[:, a:e - 1], ALU.mult, ALU.add).then_inc(tap3, 1)

            @block.gpsimd
            def _(pool):
                for h in range(MH):
                    b = h % 2
                    pool.wait_ge(u_in[b], 64 * (h // 2 + 1))
                    if h >= 2:
                        pool.wait_ge(grp_done, NG * (h - 1))
                    pool.tensor_copy(whi[b][:, :, :], wraw[b][:, :, :]).then_inc(whi_done, 1)
                    pool.wait_ge(whi_done, h + 1)
                    pool.tensor_tensor(wlo[b][:, :, :], wraw[b][:, :, :], whi[b][:, :, :].bitcast(F32), ALU.subtract).then_inc(wlo_done, 1)
                    pool.wait_ge(ahi_done, h + 1)
                    pool.tensor_tensor(alo[b][:, :, :], acc[b][:, :, :], ahi[b][:, :, :].bitcast(F32), ALU.subtract).then_inc(alo_done, 1)

            @block.scalar
            def _(act):
                def silu(h):
                    b = h % 2
                    act.wait_ge(tap3, 4 * h + 4)
                    for k in range(2):
                        act.activation(acc[b][:, k, :], acc[b][:, k, :], ACT.Silu, bias=cw[b][:, k, 3:4]).then_inc(a_done, 1)
                    act.wait_ge(a_done, 2 * h + 2)
                    if h >= 2:
                        act.wait_ge(grp_done, NG * (h - 1))
                    act.activation(ahi[b][:, :, :], acc[b][:, :, :], ACT.Copy).then_inc(ahi_done, 1)

                def store(g):
                    h, r = divmod(g, NG)
                    qk, r = divmod(r, 6)
                    m, c = divmod(r, 3)
                    act.wait_ge(evac_done, g + 1)
                    act.dma_start((d["k2"] if qk else d["q2"])[h * MD + m * P:h * MD + (m + 1) * P, c * 512:(c + 1) * 512],
                                  stage[g % 4][:, :]).then_inc(out_done[g % 4], 16)

                silu(0)
                for g in range(MH * NG):
                    if g % NG == 0 and g // NG + 1 < MH:
                        silu(g // NG + 1)
                    act.wait_ge(grp_done, g + 1)
                    if g >= 4:
                        act.wait_ge(out_done[g % 4], 16 * (g // 4))
                    act.activation(stage[g % 4][:, :], ring[g % 4][:, :], ACT.Copy,
                                   scale=MD ** -0.5 if g % NG >= 6 else 1.0).then_inc(evac_done, 1)
                    if g:
                        store(g - 1)
                store(MH * NG - 1)
                for k in range(4):
                    act.wait_ge(out_done[k], 16 * MH * NG // 4)

            @block.tensor
            def _(pe):
                for g in range(MH * NG):
                    h, r = divmod(g, NG)
                    b = h % 2
                    if r == 0:
                        pe.wait_ge(wlo_done, h + 1)
                        pe.wait_ge(alo_done, h + 1)
                    if g >= 4:
                        pe.wait_ge(evac_done, g - 3)
                    m, c = divmod(r, 3)
                    wc, tc = slice(m * P, (m + 1) * P), slice(c * 512, (c + 1) * 512)
                    for k in range(2):
                        pe.matmul(ring[g % 4][:, :], whi[b][:, k, wc], ahi[b][:, k, tc], start=(k == 0), stop=False)
                        pe.matmul(ring[g % 4][:, :], whi[b][:, k, wc], alo[b][:, k, tc], start=False, stop=False)
                        mm = pe.matmul(ring[g % 4][:, :], wlo[b][:, k, wc], ahi[b][:, k, tc], start=False, stop=(k == 1))
                    mm.then_inc(grp_done, 1)


def mlstm(nc, d):
    BW = 32
    with Stage(nc, "ml") as keep:
        ccol = keep.sb("ccol", [P, NT, 64])
        ecol = keep.sb("ecol", [P, NT, 64])

        with Stage(nc, "mg") as s:
            ident = s.sb("ident", [P, P])
            ii, ff, x, l, c, m, e = (s.sb(n, [64, T]) for n in ("ii", "ff", "x", "l", "c", "m", "e"))
            ones = s.sb("ones", [64, T])
            bias = s.sb("bias", [64, 2])
            tp = [s.ps(f"tp{k}", [P, 512]) for k in range(4)]
            const_in, z_done, chain, act_in, act_out, t_mm, col_done, m_out = (
                s.sem(n) for n in ("const_in", "z_done", "chain", "act_in", "act_out", "t_mm", "col_done", "m_out"))
            with s.block() as block:

                @block.gpsimd
                def _(pool):
                    pool.memset(ii[:, :], 0.0).then_inc(z_done, 1)
                    pool.memset(ff[:, :], 0.0).then_inc(z_done, 1)
                    pool.memset(bias[:, :], 0.0).then_inc(z_done, 1)
                    pool.memset(ones[:, :], 1.0).then_inc(z_done, 1)
                    pool.memset(x[:, :], 0.0).then_inc(z_done, 1)
                    pool.memset(c[:, :], 0.0).then_inc(z_done, 1)
                    pool.memset(m[:, :], 0.0).then_inc(z_done, 1)

                @block.sync
                def _(sp):
                    sp.dma_start(ident[:, :], d["ident"][:, :]).then_inc(const_in, 16)
                    sp.wait_ge(z_done, 3)
                    for dr in range(2):
                        r = slice(dr * BW, dr * BW + MH)
                        sp.dma_start(ii[r, :], d["gg"][8 * dr:8 * dr + MH, :]).then_inc(const_in, 16)
                        sp.dma_start(ff[r, :], d["gg"][8 * dr + MH:8 * dr + 2 * MH, :]).then_inc(const_in, 16)
                        sp.dma_start(bias[r, :], d["gate_b"][dr, :, :]).then_inc(const_in, 16)
                    sp.wait_ge(act_in, 3)
                    for dr in range(2):
                        sp.dma_start(d["mrow"][MH * dr:MH * (dr + 1), :], m[dr * BW:dr * BW + MH, :]).then_inc(m_out, 16)
                    sp.wait_ge(m_out, 32)

                @block.scalar
                def _(act):
                    act.wait_ge(act_in, 1)
                    act.activation(e[:, :], l[:, :], ACT.Exp).then_inc(act_out, 1)
                    act.wait_ge(act_in, 2)
                    act.activation(l[:, :], e[:, :], ACT.Ln).then_inc(act_out, 1)
                    act.wait_ge(act_in, 4)
                    act.activation(e[:, :], e[:, :], ACT.Exp, scale=-1.0).then_inc(act_out, 1)

                @block.vector
                def _(dve):
                    links = [0]

                    def link(ins):
                        links[0] += 1
                        ins.then_inc(chain, 1)
                        dve.wait_ge(chain, links[0])

                    dve.wait_ge(z_done, 7)
                    dve.wait_ge(const_in, 112)
                    link(dve.tensor_scalar(ff[:, :], ff[:, :], bias[:, 1:2], None, ALU.add))
                    link(dve.tensor_scalar(ii[:, :], ii[:, :], bias[:, 0:1], None, ALU.add))
                    link(dve.scalar_tensor_tensor(l[:, :], ff[:, :], -1.0, ff[:, :], ALU.mult, ALU.min))
                    dve.sem_inc(act_in, 1)
                    dve.wait_ge(act_out, 1)
                    link(dve.tensor_scalar(e[:, :], e[:, :], 1.0, None, ALU.add))
                    dve.sem_inc(act_in, 1)
                    dve.wait_ge(act_out, 2)
                    link(dve.tensor_scalar(ff[:, :], ff[:, :], 0.0, None, ALU.min))
                    link(dve.tensor_tensor(ff[:, :], ff[:, :], l[:, :], ALU.subtract))
                    runs = [(slice(dr * BW, dr * BW + MH), slice(t0, t0 + ln) if dr == 0 else slice(t0 + ln - 1, t0 - 1 if t0 else None, -1))
                            for dr in range(2) for t0, ln in SEQS]
                    for r, t in runs:
                        link(dve.tensor_tensor_scan(x[r, t], ones[r, t], ff[r, t], 0.0, ALU.mult, ALU.add))
                    link(dve.tensor_tensor(c[:, :], ii[:, :], x[:, :], ALU.subtract))
                    for r, t in runs:
                        link(dve.tensor_tensor_scan(m[r, t], c[r, t], c[r, t], 0.0, ALU.max, ALU.max))
                    dve.sem_inc(act_in, 1)
                    link(dve.tensor_tensor(e[:, :], m[:, :], x[:, :], ALU.add))
                    dve.sem_inc(act_in, 1)
                    for k in range(4):
                        dve.wait_ge(t_mm, k + 1)
                        dst, half = (ccol, ecol)[k // 2], k % 2
                        n = 8 if half == 0 else 4
                        dve.tensor_copy(dst[:, 8 * half:8 * half + n, :], tp[k][:, 0:64 * n].rearrange("p (n r) -> p n r", r=64)).then_inc(col_done, 1)

                @block.tensor
                def _(pe):
                    pe.wait_ge(const_in, 112)
                    for k in range(4):
                        src = (c, e)[k // 2]
                        pe.wait_ge(act_in, 3) if k == 0 else None
                        if k == 2:
                            pe.wait_ge(act_out, 3)
                        for n in range(8 * (k % 2), 8 if k % 2 == 0 else NT):
                            mm = pe.transpose(tp[k][:, (n % 8) * 64:(n % 8 + 1) * 64], src[:, n * P:(n + 1) * P], ident[0:64, 0:64])
                        mm.then_inc(t_mm, 1)

        with Stage(nc, "mh") as s:
            ident = s.sb("ident", [P, P])
            upto, frm = s.sb("upto", [P, P]), s.sb("from", [P, P])
            gain = [s.sb(f"gain{b}", [P, MD]) for b in range(2)]
            q = [s.sb(f"q{b}", [P, 2, T]) for b in range(2)]
            k_ = [s.sb(f"k{b}", [P, 2, T]) for b in range(2)]
            v = [s.sb(f"v{b}", [P, NT, MD + 2]) for b in range(2)]
            mb = [s.sb(f"mb{b}", [P, 2, T]) for b in range(2)]
            cs = s.sb("cs", [P, 2, NT, 2])
            md = [s.sb(f"md{u}", [P, 2, P]) for u in range(2)]
            pp = [s.sb(f"pp{j}", [P, LS + P]) for j in range(8)]
            oz = [s.sb(f"oz{u}", [P, 2, MD]) for u in range(2)]
            hh = [s.sb(f"hh{u}", [P, MD]) for u in range(2)]
            sq = s.sb("sq", [P, MD])
            st = [s.sb(f"st{u}", [P, 12]) for u in range(2)]
            yt = s.sb("yt", [P, 2, T])
            sp_ = [s.ps(f"sp{u}", [P, LS]) for u in range(2)]
            pf = [[s.ps(f"pf{u}{r}", [P, 512]) for r in range(2)] for u in range(2)]
            const_in, one_done, cs_done, md_done, s_mm, e_done, p_done, o_mm, h_done = (
                s.sem(n) for n in ("const_in", "one_done", "cs_done", "md_done", "s_mm", "e_done", "p_done", "o_mm", "h_done"))
            head_in = [s.sem(f"head_in{b}") for b in range(2)]
            oz_in = [s.sem(f"oz_in{u}") for u in range(2)]
            oz_done, den_done, r_done, hf_done, sq_done, ms_done, rt_done, rs_done, y_done, t_mm, yt_done, y_out = (
                s.sem(n) for n in ("oz_done", "den_done", "r_done", "hf_done", "sq_done", "ms_done", "rt_done", "rs_done", "y_done",
                                   "t_mm", "yt_done", "y_out"))
            per_block = [2 + (j > 0) + (j < ln // P - 1) for t0, ln in SEQS for j in range(ln // P)]

            def exps(g):
                return g // NT * sum(per_block) + sum(per_block[:g % NT])

            with s.block() as block:

                @block.sync
                def _(sp):
                    for dst, src in ((ident, d["ident"]), (upto, d["upto"]), (frm, d["downto"])):
                        sp.dma_start(dst[:, :], src[:, :]).then_inc(const_in, 16)

                    def load(h):
                        b = h % 2
                        cols = slice(h * MD, (h + 1) * MD)
                        sp.dma_start(q[b][:, :, :], d["q2"][cols, :].rearrange("(k p) t -> p k t", p=P)).then_inc(head_in[b], 16)
                        sp.dma_start(k_[b][:, :, :], d["k2"][cols, :].rearrange("(k p) t -> p k t", p=P)).then_inc(head_in[b], 16)
                        for dr in range(2):
                            sp.dma_start(mb[b][:, dr, :], d["mrow"][MH * dr + h, :].partition_broadcast(P)).then_inc(head_in[b], 16)
                        sp.dma_start(v[b][:, :, 0:MD], d["tmo"][:, cols].rearrange("(n p) c -> p n c", p=P)).then_inc(head_in[b], 16)
                        sp.dma_start(gain[b][:, :], d["o_c_norm"][cols].partition_broadcast(P)).then_inc(head_in[b], 16)

                    load(0)
                    for h in range(MH):
                        for n in range(NT):
                            g = h * NT + n
                            if g >= 2:
                                sp.wait_ge(y_done, g - 1)
                            for x in range(2):
                                sp.dma_start(oz[g % 2][:, x, :], d["tmo"][n * P:(n + 1) * P, (1 + x) * D + h * MD:(1 + x) * D + (h + 1) * MD]).then_inc(oz_in[g % 2], 16)
                            if n == 1 and h + 1 < MH:
                                load(h + 1)
                        for x in range(2):
                            sp.wait_ge(yt_done, (h + 1) * NT)
                            sp.dma_start(d["yt"][h * MD + x * P:h * MD + (x + 1) * P, :], yt[:, x, :]).then_inc(y_out, 16)
                    sp.wait_ge(y_out, 32 * MH)

                @block.gpsimd
                def _(pool):
                    for b in range(2):
                        pool.memset(v[b][:, :, MD:MD + 2], 1.0).then_inc(one_done, 1)
                    pool.wait_ge(const_in, 48)
                    for h in range(MH):
                        b = h % 2

                        def masked(n):
                            g = h * NT + n
                            if g >= 2:
                                pool.wait_ge(e_done, exps(g - 1))
                            for dr, mask in ((0, upto), (1, frm)):
                                pool.tensor_tensor(md[g % 2][:, dr, :], mb[b][:, dr, n * P:(n + 1) * P], mask[:, :], ALU.add).then_inc(md_done, 1)

                        def gate(n):
                            g = h * NT + n
                            pool.wait_ge(oz_in[g % 2], 32 * (g // 2 + 1))
                            pool.tensor_tensor(oz[g % 2][:, 0, :], oz[g % 2][:, 0, :], oz[g % 2][:, 1, :], ALU.mult).then_inc(oz_done, 1)
                            pool.wait_ge(oz_done, 2 * g + 1)
                            pool.tensor_tensor(oz[g % 2][:, 0, :], oz[g % 2][:, 0, :], gain[b][:, :], ALU.mult).then_inc(oz_done, 1)

                        pool.wait_ge(head_in[b], 96 * (h // 2 + 1))
                        for t0, ln in SEQS:
                            for n in range(t0 // P, (t0 + ln) // P):
                                masked(n)
                            for n in range(t0 // P, (t0 + ln) // P):
                                gate(n)

                @block.scalar
                def _(act):
                    for h in range(MH):
                        b = h % 2
                        act.wait_ge(head_in[b], 96 * (h // 2 + 1))
                        act.wait_ge(cs_done, 4 * (h + 1))
                        for t0, ln in SEQS:
                            nb = ln // P
                            for j in range(nb):
                                n = t0 // P + j
                                g = h * NT + n
                                if j == 0 and g:
                                    act.wait_ge(o_mm, 2 * (h * NT + t0 // P))
                                act.wait_ge(md_done, 2 * (g + 1))
                                pj, cf, cb = pp[j], cs[:, 0, n, 0:1], cs[:, 0, n, 1:2]
                                mid = (j + 1) * P
                                act.activation(pj[:, mid - P:mid], md[g % 2][:, 1, :], ACT.Exp, scale=-1.0, bias=cb).then_inc(e_done, 1)
                                act.activation(pj[:, mid:mid + P], md[g % 2][:, 0, :], ACT.Exp, scale=-1.0, bias=cf).then_inc(e_done, 1)
                                for rng, src, bias in ((slice(0, mid - P), mb[b][:, 1, t0:t0 + j * P], cb),
                                                       (slice(mid + P, ln + P), mb[b][:, 0, t0 + mid:t0 + ln], cf)):
                                    if rng.start < rng.stop:
                                        act.activation(pj[:, rng], src, ACT.Exp, scale=-1.0, bias=bias).then_inc(e_done, 1)
                            for j in range(nb):
                                n = t0 // P + j
                                g = h * NT + n
                                u = g % 2
                                act.wait_ge(hf_done, 2 * (g + 1))
                                if g:
                                    act.wait_ge(sq_done, g)
                                act.activation(sq[:, :], hh[u][:, :], ACT.Square, accum_out=st[u][:, 4:5]).then_inc(sq_done, 1)
                                act.wait_ge(ms_done, g + 1)
                                act.activation(st[u][:, 6:7], st[u][:, 5:6], ACT.Sqrt).then_inc(rt_done, 1)
                                act.wait_ge(t_mm, g + 1)
                                if n == 0 and h:
                                    act.wait_ge(y_out, 32 * h)
                                for x in range(2):
                                    ins = act.activation(yt[:, x, n * P:(n + 1) * P], pf[u][x][:, 260:260 + P], ACT.Copy)
                                ins.then_inc(yt_done, 1)

                @block.vector
                def _(dve):
                    for h in range(MH):
                        b = h % 2
                        if h:
                            dve.wait_ge(e_done, exps(NT * h))
                        for x, src in enumerate((ccol, ecol)):
                            for dr in range(2):
                                dve.tensor_copy(cs[:, x, :, dr:dr + 1], src[:, :, BW * dr + h:BW * dr + h + 1]).then_inc(cs_done, 1)
                        dve.wait_ge(cs_done, 4 * (h + 1))
                        for t0, ln in SEQS:
                            nb = ln // P
                            for j in range(nb):
                                g = h * NT + t0 // P + j
                                mid = (j + 1) * P
                                dve.wait_ge(s_mm, g + 1)
                                dve.wait_ge(e_done, exps(g + 1))
                                dve.tensor_tensor(pp[j][:, 0:mid], pp[j][:, 0:mid], sp_[g % 2][:, 0:mid], ALU.mult).then_inc(p_done, 1)
                                dve.tensor_tensor(pp[j][:, mid:ln + P], pp[j][:, mid:ln + P], sp_[g % 2][:, mid - P:ln], ALU.mult).then_inc(p_done, 1)
                            for j in range(nb):
                                n = t0 // P + j
                                g = h * NT + n
                                u = g % 2
                                w = st[u]
                                dve.wait_ge(o_mm, 2 * (g + 1))
                                for dr in range(2):
                                    dve.tensor_scalar(w[:, 8 + dr:9 + dr], pf[u][dr][:, MD:MD + 1], -1.0, cs[:, 1, n, dr:dr + 1], ALU.mult, ALU.max).then_inc(den_done, 1)
                                dve.wait_ge(den_done, 4 * g + 2)
                                for dr in range(2):
                                    dve.tensor_tensor(w[:, dr:dr + 1], w[:, 8 + dr:9 + dr], pf[u][dr][:, MD:MD + 1], ALU.max).then_inc(den_done, 1)
                                dve.wait_ge(den_done, 4 * (g + 1))
                                dve.reciprocal(w[:, 2:4], w[:, 0:2]).then_inc(r_done, 1)
                                dve.wait_ge(r_done, g + 1)
                                dve.tensor_scalar(hh[u][:, :], pf[u][0][:, 0:MD], w[:, 2:3], None, ALU.mult).then_inc(hf_done, 1)
                                dve.wait_ge(hf_done, 2 * g + 1)
                                dve.scalar_tensor_tensor(hh[u][:, :], pf[u][1][:, 0:MD], w[:, 3:4], hh[u][:, :], ALU.mult, ALU.add).then_inc(hf_done, 1)
                                dve.wait_ge(sq_done, g + 1)
                                dve.tensor_scalar(w[:, 5:6], w[:, 4:5], 1.0 / MD, EPS, ALU.mult, ALU.add).then_inc(ms_done, 1)
                                dve.wait_ge(rt_done, g + 1)
                                dve.reciprocal(w[:, 7:8], w[:, 6:7]).then_inc(rs_done, 1)
                                dve.wait_ge(rs_done, g + 1)
                                dve.wait_ge(oz_done, 2 * (g + 1))
                                dve.scalar_tensor_tensor(hh[u][:, :], hh[u][:, :], w[:, 7:8], oz[u][:, 0, :], ALU.mult, ALU.mult).then_inc(y_done, 1)

                @block.tensor
                def _(pe):
                    pe.wait_ge(const_in, 48)
                    pe.wait_ge(one_done, 2)
                    for h in range(MH):
                        b = h % 2
                        pe.wait_ge(head_in[b], 96 * (h // 2 + 1))
                        for t0, ln in SEQS:
                            nb = ln // P
                            for j in range(nb):
                                g = h * NT + t0 // P + j
                                if g >= 2:
                                    pe.wait_ge(p_done, 2 * (g - 1))
                                for c in range(ln // 512):
                                    for kk in range(2):
                                        mm = pe.matmul(sp_[g % 2][:, c * 512:(c + 1) * 512], k_[b][:, kk, t0 + j * P:t0 + (j + 1) * P],
                                                       q[b][:, kk, t0 + c * 512:t0 + (c + 1) * 512], start=(kk == 0), stop=(kk == 1))
                                mm.then_inc(s_mm, 1)

                            def turn(n):
                                g = h * NT + n
                                pe.wait_ge(y_done, g + 1)
                                for x in range(2):
                                    mm = pe.transpose(pf[g % 2][x][:, 260:260 + P], hh[g % 2][:, x * P:(x + 1) * P], ident[:, :])
                                mm.then_inc(t_mm, 1)

                            pe.wait_ge(p_done, 2 * (h * NT + t0 // P + nb))
                            for i in range(nb):
                                n = t0 // P + i
                                g = h * NT + n
                                if g >= 2:
                                    pe.wait_ge(yt_done, g - 1)
                                for dr, js in ((0, range(0, i + 1)), (1, range(i, nb))):
                                    at = (i + 1) * P if dr == 0 else i * P
                                    for j in js:
                                        mm = pe.matmul(pf[g % 2][dr][:, 0:MD + 2], pp[j][:, at:at + P], v[b][:, t0 // P + j, :],
                                                       start=(j == js[0]), stop=(j == js[-1]))
                                    mm.then_inc(o_mm, 1)
                                if i:
                                    turn(n - 1)
                            turn(t0 // P + nb - 1)


def gla(nc, d):
    CK = P
    steps = [(0, n, n + 1, n == t0 // P) for t0, ln in SEQS for n in range(t0 // P, (t0 + ln) // P - 1)]
    steps += [(1, n, n - 1, n == (t0 + ln) // P - 1) for t0, ln in SEQS for n in range((t0 + ln) // P - 1, t0 // P, -1)]
    NS = len(steps)
    with Stage(nc, "ga") as s:
        ident, m_f, m_b, ones = (s.sb(n, [P, P]) for n in ("ident", "m_f", "m_b", "ones"))
        q, k_ = s.sb("q", [P, T]), s.sb("k", [P, T])
        v = [s.sb(f"v{b}", [P, NT, GV]) for b in range(2)]
        lr = s.sb("lr", [16, 2, T])
        w2 = [s.sb(f"w2{b}", [16, 2, GK]) for b in range(2)]
        b2 = [s.sb(f"b2{b}", [P, 2]) for b in range(2)]
        gain = [s.sb(f"gain{b}", [P, GV]) for b in range(2)]
        x = [s.sb(f"x{r}", [P, T]) for r in range(2)]
        e = [s.sb(f"e{r}", [P, T]) for r in range(2)]
        q1, q2, k1, k2 = ([s.sb(f"{n}{r}", [P, T]) for r in range(2)] for n in ("q1", "q2", "k1", "k2"))
        dec = s.sb("dec", [P, 2, NT])
        state = [s.sb(f"state{r}", [P, NT, GV]) for r in range(2)]
        kt = [s.sb(f"kt{u}", [P, P]) for u in range(2)]
        am = [s.sb(f"am{u}", [P, 3, P]) for u in range(2)]
        zg = [s.sb(f"zg{u}", [P, GV]) for u in range(2)]
        y = [s.sb(f"y{u}", [P, GV]) for u in range(2)]
        yo = [s.sb(f"yo{u}", [P, 2, P]) for u in range(2)]
        sq = s.sb("sq", [P, GV])
        st = [s.sb(f"st{u}", [P, 4]) for u in range(2)]
        pa = [s.ps(f"pa{u}", [P, 512]) for u in range(2)]
        pt = [s.ps(f"pt{u}", [P, 512]) for u in range(2)]
        pkv = [s.ps(f"pkv{u}", [P, 512]) for u in range(2)]
        po = [s.ps(f"po{u}", [P, 512]) for u in range(2)]

        names = ("const_in one_done q_in lg_mm x_done na_done e_done l_done lg_done cb_done d1_done d2_done ex1 ex2 q_done k_done "
                 "kt_mm kt_done kv_mm st_done a_mm am_mul am_done o_mm sq_done ms_done rt_done rs_done zg_done y_done t_mm yo_done").split()
        sem = {n: s.sem(n) for n in names}
        v_in = [s.sem(f"v_in{b}") for b in range(2)]
        z_in = [s.sem(f"z_in{u}") for u in range(2)]
        y_out = [s.sem(f"y_out{u}") for u in range(2)]

        def chunks(t):
            return t[:, :].rearrange("p (n t) -> p n t", t=CK)

        with s.block() as block:

            @block.sync
            def _(sp):
                for dst, src in ((ident, d["ident"]), (m_f, d["m_upto"]), (m_b, d["m_from"])):
                    sp.dma_start(dst[:, :], src[:, :]).then_inc(sem["const_in"], 16)
                for dr in range(2):
                    sp.dma_start(lr[:, dr, :], d["gg"][16 + 16 * dr:32 + 16 * dr, :]).then_inc(sem["const_in"], 16)
                for h in range(GH):
                    b = h % 2
                    if h:
                        sp.wait_ge(sem["q_done"], 4 * h)
                        sp.wait_ge(sem["k_done"], 4 * h)
                    sp.dma_start(q[:, :], d["qkd"][h * GK:(h + 1) * GK, :]).then_inc(sem["q_in"], 16)
                    sp.dma_start(k_[:, :], d["qkd"][(GH + h) * GK:(GH + h + 1) * GK, :]).then_inc(sem["q_in"], 16)
                    if h >= 2:
                        sp.wait_ge(sem["o_mm"], NT * (h - 1))
                    cols = slice(3 * D + h * GV, 3 * D + (h + 1) * GV)
                    sp.dma_start(v[b][:, :, :], d["tmo"][:, cols].rearrange("(n p) c -> p n c", p=P)).then_inc(v_in[b], 16)
                    sp.dma_start(w2[b][:, :, :], d["o_w_gate2"][:, :, h * GK:(h + 1) * GK].rearrange("a r k -> r a k")).then_inc(v_in[b], 16)
                    sp.dma_start(b2[b][:, :], d["gate2_col"][h]).then_inc(v_in[b], 16)
                    if h >= 2:
                        sp.wait_ge(sem["zg_done"], NT * (h - 1))
                    sp.dma_start(gain[b][:, :], d["o_d_norm"][h * GV:(h + 1) * GV].partition_broadcast(P)).then_inc(v_in[b], 16)
                    for n in range(NT):
                        g = h * NT + n
                        if g >= 2:
                            sp.wait_ge(sem["y_done"], g - 1)
                        sp.dma_start(zg[g % 2][:, :], d["tmo"][n * P:(n + 1) * P, 4 * D + h * GV:4 * D + (h + 1) * GV]).then_inc(z_in[g % 2], 16)

            @block.gpsimd
            def _(pool):
                pool.memset(ones[:, :], 1.0).then_inc(sem["one_done"], 1)
                for h in range(GH):
                    b = h % 2
                    pool.wait_ge(sem["q_in"], 32 * (h + 1))
                    for dr in range(2):
                        pool.wait_ge(sem["ex1"], 4 * h + 2 * dr + 2)
                        pool.tensor_tensor(k1[dr][:, :], k1[dr][:, :], k_[:, :], ALU.mult).then_inc(sem["k_done"], 1)
                        pool.wait_ge(sem["ex2"], 6 * h + 3 * dr + 3)
                        pool.tensor_tensor(k2[dr][:, :], k2[dr][:, :], k_[:, :], ALU.mult).then_inc(sem["k_done"], 1)
                    pool.wait_ge(v_in[b], 64 * (h // 2 + 1))
                    for n in range(NT):
                        g = h * NT + n
                        pool.wait_ge(z_in[g % 2], 16 * (g // 2 + 1))
                        pool.tensor_tensor(zg[g % 2][:, :], zg[g % 2][:, :], gain[b][:, :], ALU.mult).then_inc(sem["zg_done"], 1)

            @block.scalar
            def _(act):
                for h in range(GH):
                    for dr in range(2):
                        i = 2 * h + dr
                        act.wait_ge(sem["na_done"], i + 1)
                        act.activation(e[dr][:, :], e[dr][:, :], ACT.Exp).then_inc(sem["e_done"], 1)
                        act.wait_ge(sem["e_done"], i + 1)
                        act.activation(e[dr][:, :], e[dr][:, :], ACT.Ln, bias=1.0).then_inc(sem["l_done"], 1)
                    if h:
                        act.wait_ge(sem["o_mm"], NT * h)
                    for dr in range(2):
                        i = 2 * h + dr
                        end = CK - 1 if dr == 0 else 0
                        act.wait_ge(sem["d1_done"], i + 1)
                        act.activation(q1[dr][:, :], e[dr][:, :], ACT.Exp, scale=1 / 16).then_inc(sem["ex1"], 1)
                        act.activation(k1[dr][:, :], e[dr][:, :], ACT.Exp, scale=-1 / 16).then_inc(sem["ex1"], 1)
                        act.activation(q2[dr][:, :], x[dr][:, :], ACT.Exp, scale=1 / 16).then_inc(sem["ex2"], 1)
                        act.activation(dec[:, dr, :], chunks(x[dr])[:, :, end], ACT.Exp, scale=1 / 16).then_inc(sem["ex2"], 1)
                        act.wait_ge(sem["d2_done"], i + 1)
                        act.activation(k2[dr][:, :], e[dr][:, :], ACT.Exp, scale=-1 / 16).then_inc(sem["ex2"], 1)
                    for m in range(NS):
                        g = h * NS + m
                        act.wait_ge(sem["kt_mm"], g + 1)
                        if g >= 2:
                            act.wait_ge(sem["kv_mm"], g - 1)
                        act.activation(kt[g % 2][:, :], pt[g % 2][:, 0:P], ACT.Copy).then_inc(sem["kt_done"], 1)
                    for n in range(NT):
                        g = h * NT + n
                        u = g % 2
                        act.wait_ge(sem["o_mm"], g + 1)
                        if g:
                            act.wait_ge(sem["sq_done"], g)
                        act.activation(sq[:, :], po[u][:, 0:GV], ACT.Square, accum_out=st[u][:, 0:1]).then_inc(sem["sq_done"], 1)
                        act.wait_ge(sem["ms_done"], g + 1)
                        act.activation(st[u][:, 2:3], st[u][:, 1:2], ACT.Sqrt).then_inc(sem["rt_done"], 1)
                        act.wait_ge(sem["t_mm"], g + 1)
                        if g >= 2:
                            act.wait_ge(y_out[u], 32 * (g // 2))
                        act.activation(yo[u][:, :, :], po[u][:, GV:2 * GV].rearrange("p (a b) -> p a b", a=2), ACT.Copy).then_inc(sem["yo_done"], 1)
                        act.wait_ge(sem["yo_done"], g + 1)
                        for a in range(2):
                            act.dma_start(d["yt"][D + h * GV + a * P:D + h * GV + (a + 1) * P, n * P:(n + 1) * P], yo[u][:, a, :]).then_inc(y_out[u], 16)
                for u in range(2):
                    act.wait_ge(y_out[u], 32 * GH * NT // 2)

            @block.vector
            def _(dve):
                dve.wait_ge(sem["one_done"], 1)
                dve.wait_ge(sem["const_in"], 80)
                for h in range(GH):
                    b = h % 2
                    dve.wait_ge(v_in[b], 64 * (h // 2 + 1))
                    for dr in range(2):
                        if h and dr == 0:
                            dve.wait_ge(sem["ex2"], 6 * h)
                        for c in range(3):
                            m = 6 * h + 3 * dr + c
                            dve.wait_ge(sem["lg_mm"], m + 1)
                            dve.tensor_scalar(x[dr][:, c * 512:(c + 1) * 512], pa[m % 2][:, :], b2[b][:, dr:dr + 1], None, ALU.add).then_inc(sem["x_done"], 1)
                        dve.wait_ge(sem["x_done"], 6 * h + 3 * dr + 3)
                        dve.scalar_tensor_tensor(e[dr][:, :], x[dr][:, :], -1.0, x[dr][:, :], ALU.mult, ALU.min).then_inc(sem["na_done"], 1)
                    for dr in range(2):
                        i = 2 * h + dr
                        dve.wait_ge(sem["l_done"], i + 1)
                        dve.scalar_tensor_tensor(e[dr][:, :], x[dr][:, :], 0.0, e[dr][:, :], ALU.min, ALU.subtract).then_inc(sem["lg_done"], 1)
                        dve.wait_ge(sem["lg_done"], i + 1)
                        for n in range(NT):
                            t = slice(n * P, (n + 1) * P) if dr == 0 else slice((n + 1) * P - 1, n * P - 1 if n else None, -1)
                            dve.tensor_tensor_scan(x[dr][:, t], ones[:, :], e[dr][:, t], 0.0, ALU.mult, ALU.add).then_inc(sem["cb_done"], 1)
                        mid, end = (CK // 2 - 1, CK - 1) if dr == 0 else (CK // 2, 0)
                        cb = chunks(x[dr])
                        dve.wait_ge(sem["cb_done"], NT * (i + 1))
                        dve.tensor_tensor(chunks(e[dr]), cb, cb[:, :, mid:mid + 1].broadcast_to([P, NT, CK]), ALU.subtract).then_inc(sem["d1_done"], 1)
                        dve.wait_ge(sem["ex1"], 2 * (i + 1))
                        dve.tensor_tensor(chunks(e[dr]), cb, cb[:, :, end:end + 1].broadcast_to([P, NT, CK]), ALU.subtract).then_inc(sem["d2_done"], 1)
                        if dr == 0:
                            dve.wait_ge(sem["q_in"], 32 * (h + 1))
                        dve.scalar_tensor_tensor(q1[dr][:, :], q[:, :], GK ** -0.5, q1[dr][:, :], ALU.mult, ALU.mult).then_inc(sem["q_done"], 1)
                        dve.wait_ge(sem["ex2"], 6 * h + 3 * dr + 1)
                        dve.scalar_tensor_tensor(q2[dr][:, :], q[:, :], GK ** -0.5, q2[dr][:, :], ALU.mult, ALU.mult).then_inc(sem["q_done"], 1)
                    dve.wait_ge(sem["ex2"], 6 * (h + 1))
                    for m, (dr, n, nx, first) in enumerate(steps):
                        g = h * NS + m
                        dve.wait_ge(sem["kv_mm"], g + 1)
                        if first:
                            dve.tensor_copy(state[dr][:, nx, :], pkv[g % 2][:, 0:GV]).then_inc(sem["st_done"], 1)
                        else:
                            dve.wait_ge(sem["st_done"], g)
                            dve.scalar_tensor_tensor(state[dr][:, nx, :], state[dr][:, n, :], dec[:, dr, n:n + 1], pkv[g % 2][:, 0:GV],
                                                     ALU.mult, ALU.add).then_inc(sem["st_done"], 1)

                    def weights(n):
                        g = h * NT + n
                        u = g % 2
                        dve.wait_ge(sem["a_mm"], g + 1)
                        if g >= 2:
                            dve.wait_ge(sem["o_mm"], g - 1)
                        dve.tensor_tensor(am[u][:, 0, :], pa[u][:, 0:P], m_f[:, :], ALU.mult).then_inc(sem["am_mul"], 1)
                        dve.tensor_tensor(am[u][:, 1, :], pa[u][:, P:2 * P], m_b[:, :], ALU.mult).then_inc(sem["am_mul"], 1)
                        dve.wait_ge(sem["am_mul"], 2 * (g + 1))
                        dve.tensor_tensor(am[u][:, 2, :], am[u][:, 0, :], am[u][:, 1, :], ALU.add).then_inc(sem["am_done"], 1)

                    weights(0)
                    for n in range(NT):
                        if n + 1 < NT:
                            weights(n + 1)
                        g = h * NT + n
                        w = st[g % 2]
                        dve.wait_ge(sem["sq_done"], g + 1)
                        dve.tensor_scalar(w[:, 1:2], w[:, 0:1], 1.0 / GV, EPS, ALU.mult, ALU.add).then_inc(sem["ms_done"], 1)
                        dve.wait_ge(sem["rt_done"], g + 1)
                        dve.reciprocal(w[:, 3:4], w[:, 2:3]).then_inc(sem["rs_done"], 1)
                        dve.wait_ge(sem["rs_done"], g + 1)
                        dve.wait_ge(sem["zg_done"], g + 1)
                        if g >= 2:
                            dve.wait_ge(sem["t_mm"], g - 1)
                        dve.scalar_tensor_tensor(y[g % 2][:, :], po[g % 2][:, 0:GV], w[:, 3:4], zg[g % 2][:, :], ALU.mult, ALU.mult).then_inc(sem["y_done"], 1)

            @block.tensor
            def _(pe):
                pe.wait_ge(sem["const_in"], 80)
                for h in range(GH):
                    b = h % 2
                    pe.wait_ge(v_in[b], 64 * (h // 2 + 1))
                    if h:
                        pe.wait_ge(sem["am_done"], NT * h)
                    for m in range(6):
                        g = 6 * h + m
                        dr, c = divmod(m, 3)
                        if m >= 2:
                            pe.wait_ge(sem["x_done"], g - 1)
                        pe.matmul(pa[g % 2][:, :], w2[b][:, dr, :], lr[:, dr, c * 512:(c + 1) * 512], start=True, stop=True).then_inc(sem["lg_mm"], 1)

                    pe.wait_ge(sem["k_done"], 4 * (h + 1))
                    pe.wait_ge(sem["q_done"], 4 * (h + 1))

                    def flip(m):
                        g = h * NS + m
                        dr, n = steps[m][:2]
                        if g >= 2:
                            pe.wait_ge(sem["kt_done"], g - 1)
                        pe.transpose(pt[g % 2][:, 0:P], k2[dr][:, n * P:(n + 1) * P], ident[:, :]).then_inc(sem["kt_mm"], 1)

                    flip(0)
                    for m, (dr, n, nx, first) in enumerate(steps):
                        g = h * NS + m
                        if m + 1 < NS:
                            flip(m + 1)
                        pe.wait_ge(sem["kt_done"], g + 1)
                        if g >= 2:
                            pe.wait_ge(sem["st_done"], g - 1)
                        pe.matmul(pkv[g % 2][:, 0:GV], kt[g % 2][:, :], v[b][:, n, :], start=True, stop=True).then_inc(sem["kv_mm"], 1)

                    def weights(n):
                        g = h * NT + n
                        if n < 2:
                            pe.wait_ge(sem["x_done"], 6 * (h + 1))
                        if g >= 2:
                            pe.wait_ge(sem["am_done"], g - 1)
                        for dr in range(2):
                            mm = pe.matmul(pa[g % 2][:, dr * P:(dr + 1) * P], k1[dr][:, n * P:(n + 1) * P], q1[dr][:, n * P:(n + 1) * P],
                                           start=True, stop=True)
                        mm.then_inc(sem["a_mm"], 1)

                    def turn(n):
                        g = h * NT + n
                        pe.wait_ge(sem["y_done"], g + 1)
                        for a in range(2):
                            mm = pe.transpose(po[g % 2][:, GV + a * P:GV + (a + 1) * P], y[g % 2][:, a * P:(a + 1) * P], ident[:, :])
                        mm.then_inc(sem["t_mm"], 1)

                    weights(0)
                    pe.wait_ge(sem["st_done"], NS * (h + 1))
                    for n in range(NT):
                        g = h * NT + n
                        u = g % 2
                        if n + 1 < NT:
                            weights(n + 1)
                        pe.wait_ge(sem["am_done"], g + 1)
                        if g >= 2:
                            pe.wait_ge(sem["yo_done"], g - 1)
                        parts = [(am[u][:, 2, :], v[b][:, n, :])]
                        tc = slice(n * P, (n + 1) * P)
                        if n not in (0, LP // P):
                            parts.append((q2[0][:, tc], state[0][:, n, :]))
                        if n not in (LP // P - 1, NT - 1):
                            parts.append((q2[1][:, tc], state[1][:, n, :]))
                        for i, (lhs, rhs) in enumerate(parts):
                            mm = pe.matmul(po[u][:, 0:GV], lhs, rhs, start=(i == 0), stop=(i == len(parts) - 1))
                        mm.then_inc(sem["o_mm"], 1)
                        if n:
                            turn(n - 1)
                    turn(NT - 1)


def odd_out_projection(nc, d):
    out_projection(nc, d, "oo", d["o_w_out"], d["post_norm"][1],
                   ((d["x1"][0:LP, :], d["y_prompt"], 0, LP // P), (d["x1"][LP:T, :], d["y_sample"], LP // P, LS // P)))


def odd_layer(nc, d):
    odd_input_projection(nc, d)
    conv_and_qk(nc, d)
    mlstm(nc, d)
    gla(nc, d)
    odd_out_projection(nc, d)

SCRATCH_KIND = "Internal"


INPUTS = {
    "x_prompt": (1, LP, D), "x_sample": (1, LS, D), "pre_norm": (2, D), "post_norm": (2, D),
    "e_w_in": (1, D, IN_EVEN), "e_lam_re": (1, 2, G5, ST), "e_lam_im": (1, 2, G5, ST), "e_log_dt": (1, 2, G5),
    "e_b_re": (1, 2, G5, ST, GC), "e_b_im": (1, 2, G5, ST, GC), "e_c_re": (1, 2, G5, GC, ST),
    "e_c_im": (1, 2, G5, GC, ST), "e_d_skip": (1, D), "e_w_glu": (1, D, D), "e_q_norm": (1, QL),
    "e_w_uq": (1, QL, HEADS * (NOPE + ROPE)), "e_kv_norm": (1, KVL), "e_w_ukv": (1, KVL, HEADS * (NOPE + VD)),
    "e_w_out": (1, 2 * D, D), "o_w_in": (1, D, IN_ODD), "o_conv_w": (1, 3, D), "o_conv_b": (1, D),
    "o_w_q": (1, MH, MD, MD), "o_w_k": (1, MH, MD, MD), "o_gate_b": (1, 16), "o_c_norm": (1, D),
    "o_w_gate2": (1, 2, 16, GH * GK), "o_gate2_b": (1, 2, GH * GK), "o_d_norm": (1, D), "o_w_out": (1, 2 * D, D),
}
SCRATCH = {
    "u_s": (NCS, G5, CH, GC), "u_p": (NCP, G5, CH, GC),
    "za": (D, T), "zb": (D, T), "cq": (T, CW), "gt": (D, T), "yt": (2 * D, T), "x1": (T, D),
    "qn": (HEADS * NOPE, T), "qr": (HEADS * ROPE, T), "kn": (HEADS * NOPE, T), "kr": (P, T), "v": (T, HEADS * VD),
    "uc": (D, T), "tmo": (T, 5 * D), "qkd": (D, T), "at": (D, T), "lagrow": (G5, GC, 15 * GC), "cpow": (8, P, 2 * 2 * 4 * (CH + 1) * GC), "utd": (G5 // 2, P, 2 * (NCS + NCP)),
    "hst": (8, P, 2 * 2 * 4 * (NCS + NCP)), "gg": (P, T), "mrow": (8, T), "q2": (D, T), "k2": (D, T),
}


def constants():
    i = np.arange(P)
    pos = np.concatenate([np.arange(LP), np.arange(LS)]).astype(np.float32)
    inv = (np.float32(10000.0) ** (-np.arange(0, ROPE, 2, dtype=np.float32) / np.float32(ROPE))).astype(np.float32)
    ang = (pos[:, None] * inv[None, :]).astype(np.float64)
    cos, sin = np.cos(ang).astype(np.float32), np.sin(ang).astype(np.float32)
    half = np.concatenate([cos, cos], 1), np.concatenate([-sin, sin], 1)
    return {
        "ident": np.eye(P, dtype=np.float32),
        "rope_tm": np.concatenate(half, 1),
        "rope_fm": np.stack([np.tile(h.T, (2, 1)) for h in half]),
        "upto": np.where(i[:, None] <= i[None, :], 0.0, 1e30).astype(np.float32),
        "downto": np.where(i[:, None] >= i[None, :], 0.0, 1e30).astype(np.float32),
        "m_upto": (i[:, None] <= i[None, :]).astype(np.float32),
        "m_from": (i[:, None] >= i[None, :]).astype(np.float32),
    }


def laid_out(a):
    def columns(v):
        return v.reshape(v.shape[0], -1, P).transpose(0, 2, 1)

    def state_major(v):
        v = v[0].reshape(2, G5 // 2, 2, ST, -1)
        return v.transpose(2, 3, 0, 1, 4).reshape(P, 2, G5 // 2, -1)

    uq = a["e_w_uq"][0].reshape(QL, HEADS, NOPE + ROPE)
    rope = uq[:, :, NOPE:]
    return {
        "pre_col": columns(a["pre_norm"]),
        "qn_col": columns(a["e_q_norm"])[0], "kvn_col": columns(a["e_kv_norm"])[0],
        "lam_re": state_major(a["e_lam_re"])[..., 0], "lam_im": state_major(a["e_lam_im"])[..., 0],
        "log_dt": state_major(np.repeat(a["e_log_dt"][..., None], ST, 3))[..., 0],
        "b_re": state_major(a["e_b_re"]), "b_im": state_major(a["e_b_im"]),
        "c_re": state_major(a["e_c_re"].transpose(0, 1, 2, 4, 3)), "c_im": state_major(a["e_c_im"].transpose(0, 1, 2, 4, 3)),
        "d_skip": a["e_d_skip"].reshape(G5, GC).T,
        "w_uq_nope": uq[:, :, :NOPE].reshape(QL, -1), "w_uq_rope": rope.reshape(QL, -1),
        "w_uq_swap": np.concatenate([rope[:, :, ROPE // 2:], rope[:, :, :ROPE // 2]], 2).reshape(QL, -1),
        "conv_col": columns(np.concatenate([a["o_conv_w"][0], a["o_conv_b"]])).transpose(1, 2, 0),
        "gate_w": gate_columns(a["o_w_in"][0]), "gate_b": a["o_gate_b"][0].reshape(2, 2, MH).transpose(0, 2, 1),
        "gate2_col": a["o_gate2_b"][0].reshape(2, GH, GK).transpose(1, 2, 0),
    }


def gate_columns(w):
    out = np.zeros((D, P), np.float32)
    out[:, 0:16] = w[:, O_G:O_G + 16]
    out[:, 16:48] = w[:, O_LR:O_LR + 32]
    return out


def build(nc, d):
    even_layer(nc, d)
    odd_layer(nc, d)


def kernel(**inputs):
    import concourse.bacc as _bacc
    from concourse.bass_utils import run_bass_kernel_spmd as _run

    nc = _bacc.Bacc("TRN2", target_bir_lowering=False, num_devices=1)
    tensors, arrays = {}, {}
    for name, shape in INPUTS.items():
        inputs[name] = arrays[name] = np.ascontiguousarray(inputs[name])
        t = nc.dram_tensor(name, shape, F32, kind="ExternalInput").ap()
        tensors[name] = t[0] if shape[0] == 1 else t
    for name, value in laid_out(inputs).items():
        arrays["l_" + name] = np.ascontiguousarray(value)
        tensors[name] = nc.dram_tensor("l_" + name, value.shape, F32, kind="ExternalInput").ap()
    for name, value in constants().items():
        arrays["c_" + name] = value
        tensors[name] = nc.dram_tensor("c_" + name, value.shape, F32, kind="ExternalInput").ap()
    for name, shape in SCRATCH.items():
        tensors[name] = nc.dram_tensor("s_" + name, shape, F32, kind=SCRATCH_KIND).ap()
    tensors["y_prompt"] = nc.dram_tensor("y_prompt", (LP, D), F32, kind="ExternalOutput").ap()
    tensors["y_sample"] = nc.dram_tensor("y_sample", (LS, D), F32, kind="ExternalOutput").ap()
    build(nc, tensors)
    r = _run(nc, [arrays], core_ids=[0])
    return (r.results[0]["y_prompt"].reshape(1, LP, D), r.results[0]["y_sample"].reshape(1, LS, D))
```
